# Optimizing a Trainium2 kernel written in Bass

```python
import jax, jax.numpy as jnp
from jax import lax
import numpy as np

'''Two-layer bidirectional hybrid encoder trunk with parallel head groups (Hymba-style).

Inputs:  x (BATCH, SEQ, D_MODEL) float32 plus per-layer parameters stacked on a leading DEPTH axis.
Output:  (BATCH, SEQ, D_MODEL).
Each layer: one combined input projection of the normalised stream, partitioned into four head groups
(A: windowed GQA + sink + ALiBi, B: gated short conv, C: Fourier mixing, D: QK-normed GQA with 2-D axial
rotary), per-group RMS-normalised outputs concatenated into one output projection, DeepNorm post-LN
residual, then a squared-ReLU MLP with DeepNorm post-LN residual.
'''

D_MODEL = 1024
BATCH = 1
SEQ = 512
DEPTH = 2

HEAD_DIM = 64
N_GROUPS = 4
GROUP_WIDTH = D_MODEL // N_GROUPS
D_MIX = N_GROUPS * GROUP_WIDTH
A_Q_HEADS = GROUP_WIDTH // HEAD_DIM
A_KV_HEADS = 2
D_Q_HEADS = GROUP_WIDTH // HEAD_DIM
D_KV_HEADS = 2
B_HEADS = GROUP_WIDTH // HEAD_DIM
C_HEADS = GROUP_WIDTH // HEAD_DIM
CONV_WIDTH = 3
WINDOW = 128
BLOCK = 128
GRID_W = 64
AXIS_DIM = HEAD_DIM // 2
ROPE_THETA = 10000.0
D_FF = 4 * D_MODEL
LN_EPS = 1e-5
RMS_EPS = 1e-6
DN_ALPHA = (2 * DEPTH) ** 0.25
DN_BETA = (8 * DEPTH) ** -0.25
NEG_INF = -1e30
SPLIT_SIZES = (
    A_Q_HEADS * HEAD_DIM, A_KV_HEADS * HEAD_DIM, A_KV_HEADS * HEAD_DIM,
    GROUP_WIDTH, GROUP_WIDTH, GROUP_WIDTH,
    GROUP_WIDTH,
    D_Q_HEADS * HEAD_DIM, D_KV_HEADS * HEAD_DIM, D_KV_HEADS * HEAD_DIM,
)
D_IN_PROJ = 2048

kernel_name = 'hymba_style_hybrid_encoder'

def layer_norm(x, g, b):
    xf = x.astype(jnp.float32)
    mu = jnp.mean(xf, axis=-1, keepdims=True)
    var = jnp.mean(jnp.square(xf - mu), axis=-1, keepdims=True)
    return ((xf - mu) * lax.rsqrt(var + LN_EPS) * g + b).astype(x.dtype)

def rms_norm(x, g):
    xf = x.astype(jnp.float32)
    return (xf * lax.rsqrt(jnp.mean(jnp.square(xf), axis=-1, keepdims=True) + RMS_EPS) * g).astype(x.dtype)

def split_columns(h):
    parts, start = [], 0
    for size in SPLIT_SIZES:
        parts.append(h[..., start:start + size])
        start += size
    return parts

def split_heads(t, n_heads):
    return t.reshape(t.shape[0], t.shape[1], n_heads, HEAD_DIM)

def windowed_gqa_sink(q, k, v, sink):
    b_, s_, hq, hd = q.shape
    hkv = k.shape[2]
    g_ = hq // hkv
    nblk = s_ // BLOCK
    qb = q.reshape(b_, nblk, BLOCK, hkv, g_, hd)

    def windows(t):
        tp = jnp.pad(t, ((0, 0), (BLOCK, BLOCK), (0, 0), (0, 0))).reshape(b_, nblk + 2, BLOCK, hkv, hd)
        return jnp.concatenate([tp[:, :-2], tp[:, 1:-1], tp[:, 2:]], axis=2)

    kw, vw = windows(k), windows(v)
    scores = jnp.einsum('bnqkgd,bnskd->bnkgqs', qb, kw, preferred_element_type=jnp.float32) * (hd ** -0.5)
    q_pos = jnp.arange(s_).reshape(nblk, BLOCK)
    k_pos = (jnp.arange(nblk)[:, None] - 1) * BLOCK + jnp.arange(3 * BLOCK)[None, :]
    dist = jnp.abs(q_pos[:, :, None] - k_pos[:, None, :])
    valid = (dist <= WINDOW) & ((k_pos >= 0) & (k_pos < s_))[:, None, :]
    slopes = jnp.exp2(-8.0 * jnp.arange(1, hq + 1, dtype=jnp.float32) / hq).reshape(hkv, g_)
    bias = -slopes[None, :, :, None, None] * dist.astype(jnp.float32)[:, None, None, :, :]
    scores = jnp.where(valid[:, None, None], scores + bias, NEG_INF)
    sink_col = jnp.broadcast_to(sink.astype(jnp.float32).reshape(hkv, g_, 1, 1), scores.shape[:-1] + (1,))
    probs = jax.nn.softmax(jnp.concatenate([scores, sink_col], axis=-1), axis=-1)[..., :-1]
    out = jnp.einsum('bnkgqs,bnskd->bnqkgd', probs.astype(v.dtype), vw)
    return out.reshape(b_, s_, hq * hd)

def short_conv_mixer(u, gate_b, gate_c, conv_w):
    z = gate_c * u
    y = lax.conv_general_dilated(
        z, conv_w[:, None, :], window_strides=(1,),
        padding=((CONV_WIDTH // 2, CONV_WIDTH // 2),),
        dimension_numbers=('NWC', 'WIO', 'NWC'),
        feature_group_count=z.shape[-1])
    return gate_b * y

def fourier_mixer(u):
    b_, s_, c_ = u.shape
    ug = u.astype(jnp.float32).reshape(b_, s_, C_HEADS, c_ // C_HEADS)
    y = jnp.fft.fft2(ug, axes=(1, 3), norm='ortho').real
    return y.reshape(b_, s_, c_).astype(u.dtype)

def rotate_half_axis(seg, ang):
    m = ang.shape[-1]
    c = jnp.cos(ang)[None, :, None, :]
    s = jnp.sin(ang)[None, :, None, :]
    x1, x2 = seg[..., :m], seg[..., m:]
    return jnp.concatenate([x1 * c - x2 * s, x2 * c + x1 * s], axis=-1)

def axial_rope(t, ang_row, ang_col):
    tf = t.astype(jnp.float32)
    out = jnp.concatenate([rotate_half_axis(tf[..., :AXIS_DIM], ang_row),
                           rotate_half_axis(tf[..., AXIS_DIM:], ang_col)], axis=-1)
    return out.astype(t.dtype)

def dense_gqa_blocks(q, k, v):
    b_, s_, hq, hd = q.shape
    hkv = k.shape[2]
    g_ = hq // hkv
    nblk = s_ // BLOCK
    qb = q.reshape(b_, nblk, BLOCK, hkv, g_, hd).transpose(1, 0, 2, 3, 4, 5)

    def one_block(q_blk):
        sc = jnp.einsum('bqkgd,bskd->bkgqs', q_blk, k, preferred_element_type=jnp.float32) * (hd ** -0.5)
        p = jax.nn.softmax(sc, axis=-1)
        return jnp.einsum('bkgqs,bskd->bqkgd', p.astype(v.dtype), v)

    out = lax.map(one_block, qb)
    return out.transpose(1, 0, 2, 3, 4, 5).reshape(b_, s_, hq * hd)

def setup_inputs(seed: int = 0) -> dict:
    key = jax.random.key(seed)
    ks = jax.random.split(key, 16)
    f32 = jnp.float32
    nrm = lambda k, shape: jax.random.normal(k, shape, dtype=f32)
    return {
        'x': nrm(ks[0], (BATCH, SEQ, D_MODEL)),
        'ln_in_g': 1.0 + 0.02 * nrm(ks[1], (D_MODEL,)),
        'ln_in_b': 0.02 * nrm(ks[2], (D_MODEL,)),
        'w_in': nrm(ks[3], (DEPTH, D_MODEL, D_IN_PROJ)) * D_MODEL ** -0.5,
        'conv_w': nrm(ks[4], (DEPTH, CONV_WIDTH, GROUP_WIDTH)) * CONV_WIDTH ** -0.5,
        'sink': 0.5 * nrm(ks[5], (DEPTH, A_Q_HEADS)),
        'qn_g': 1.0 + 0.02 * nrm(ks[6], (DEPTH, HEAD_DIM)),
        'kn_g': 1.0 + 0.02 * nrm(ks[7], (DEPTH, HEAD_DIM)),
        'grp_g': 1.0 + 0.02 * nrm(ks[8], (DEPTH, D_MIX)),
        'w_out': nrm(ks[9], (DEPTH, D_MIX, D_MODEL)) * (D_MIX ** -0.5) * DN_BETA,
        'ln1_g': 1.0 + 0.02 * nrm(ks[10], (DEPTH, D_MODEL)),
        'ln1_b': 0.02 * nrm(ks[11], (DEPTH, D_MODEL)),
        'w1': nrm(ks[12], (DEPTH, D_MODEL, D_FF)) * (D_MODEL ** -0.5) * DN_BETA,
        'w2': nrm(ks[13], (DEPTH, D_FF, D_MODEL)) * (D_FF ** -0.5) * DN_BETA,
        'ln2_g': 1.0 + 0.02 * nrm(ks[14], (DEPTH, D_MODEL)),
        'ln2_b': 0.02 * nrm(ks[15], (DEPTH, D_MODEL)),
    }

def reference(x, ln_in_g, ln_in_b, w_in, conv_w, sink, qn_g, kn_g, grp_g, w_out,
              ln1_g, ln1_b, w1, w2, ln2_g, ln2_b):
    f32 = jnp.float32
    b_, s_, _ = x.shape
    rows = s_ // GRID_W
    row_idx = jnp.repeat(jnp.arange(rows), GRID_W)
    col_idx = jnp.tile(jnp.arange(GRID_W), rows)
    inv_freq = ROPE_THETA ** (-jnp.arange(0, AXIS_DIM, 2, dtype=f32) / AXIS_DIM)
    ang_row = row_idx.astype(f32)[:, None] * inv_freq[None, :]
    ang_col = col_idx.astype(f32)[:, None] * inv_freq[None, :]

    h = layer_norm(x, ln_in_g, ln_in_b)
    for l in range(DEPTH):
        proj = h @ w_in[l]
        a_q, a_k, a_v, b_u, b_b, b_c, c_u, d_q, d_k, d_v = split_columns(proj)
        out_a = windowed_gqa_sink(split_heads(a_q, A_Q_HEADS), split_heads(a_k, A_KV_HEADS),
                                  split_heads(a_v, A_KV_HEADS), sink[l])
        out_b = short_conv_mixer(b_u, b_b, b_c, conv_w[l])
        out_c = fourier_mixer(c_u)
        qd = axial_rope(rms_norm(split_heads(d_q, D_Q_HEADS), qn_g[l]), ang_row, ang_col)
        kd = axial_rope(rms_norm(split_heads(d_k, D_KV_HEADS), kn_g[l]), ang_row, ang_col)
        out_d = dense_gqa_blocks(qd, kd, split_heads(d_v, D_KV_HEADS))
        g = grp_g[l]
        mix = jnp.concatenate(
            [rms_norm(o, g[i * GROUP_WIDTH:(i + 1) * GROUP_WIDTH])
             for i, o in enumerate((out_a, out_b, out_c, out_d))], axis=-1)
        h = layer_norm(DN_ALPHA * h + mix @ w_out[l], ln1_g[l], ln1_b[l])
        ffn = jnp.square(jax.nn.relu(h @ w1[l])) @ w2[l]
        h = layer_norm(DN_ALPHA * h + ffn, ln2_g[l], ln2_b[l])
    return h


_drawn_inputs = setup_inputs


def setup_inputs(seed=0):
    import zlib

    import numpy as np

    out = dict(_drawn_inputs(seed))
    spreads = {}
    factors = {'sink': 8.0, 'qn_g': 8.0, 'kn_g': 8.0, 'grp_g': 5.751}
    for name, (base, spread) in spreads.items():
        noise = np.random.default_rng([zlib.crc32(name.encode()), seed]).standard_normal(out[name].shape)
        drawn = base * np.exp(spread * noise) if base else spread * noise
        out[name] = __import__('jax').numpy.asarray(drawn.astype(out[name].dtype))
    for name, factor in factors.items():
        out[name] = (out[name] * factor).astype(out[name].dtype)
    return out
```

```python
import math
from contextlib import ExitStack

import numpy as np

import concourse.bass as bass
from concourse import mybir

F32 = mybir.dt.float32
F32R = mybir.dt.float32r
ALU = mybir.AluOpType
ACT = mybir.ActivationFunctionType
AX_X = mybir.AxisListType.X

P = 128
D_MODEL = 1024
SEQ = 512
DEPTH = 2
HEAD_DIM = 64
GROUP = 256
D_FF = 4 * D_MODEL
WINDOW = 128
GRID_W = 64
AXIS_DIM = HEAD_DIM // 2
ROPE_THETA = 10000.0
LN_EPS = 1e-5
RMS_EPS = 1e-6
ALPHA = (2 * DEPTH) ** 0.25
A_HEADS = 4

TOK = SEQ // P
KT = D_MODEL // P
BANK = 512
BLOCK = 2048
RAW = 2
RING = 4
IN_BLOCKS = 2 * D_MODEL // (BLOCK // KT)
OUT_BLOCKS = 4
CHUNKS = 4
CHUNK_BLOCKS = 8
MLP0 = IN_BLOCKS + OUT_BLOCKS
BLOCKS = MLP0 + CHUNKS * CHUNK_BLOCKS
MLP_G0 = 48
CHUNK_G = 16
QK = GROUP + P
QK_HEADS = QK // HEAD_DIM
UNITS = 32
HALF = SEQ // 2 + 1

COL_PRE_G, COL_PRE_B, COL_LN1_G, COL_LN1_B = 0, 8, 16, 24
COL_CONV, COL_GRP, COL_SINK = 32, 38, 46
N_COLS = 50

PER_LAYER = dict(
    w_hi=BLOCKS, w_lo=BLOCKS, products=MLP_G0 + CHUNKS * CHUNK_G,
    turned=2 * KT, y_ready=2 * KT, h_hi=2 * KT, h_lo=2 * KT,
    stats=16, moments=8, var_ready=8, rstd=8, normed=8, gained=8, scaled=8, rows=64, row_ready=2,
    param=32,
    qk_gain=TOK, qk_square=TOK, dv_copied=TOK, qk_sum=TOK, qk_eps=TOK, qk_rstd=1, qk_unit=TOK,
    rope_cos=TOK, rope_sin=2 * TOK, qk_roped=TOK, tk_copied=TOK, aq_copied=2, bu_copied=2,
    conv_step=8, conv_out=2, group_square=8, mix_hi=8, mix_lo=8, square_sum=4, square_mean=4, group_rstd=4,
    qk_turned=4, q_copied=2, k_copied=2, freq=2, freq_copied=2, mixed=2, sine_copied=2, fourier_step=4, fourier_out=2,
    scores=UNITS, biased=16, row_max=UNITS, neg_max=UNITS, sink_exp=16, probs=UNITS, denom=16,
    inv_denom=UNITS, prob_scaled=UNITS, prob_turned=UNITS, prob_copied=UNITS, attended=UNITS,
    added=4 * 8 + CHUNKS * 8, relu=32, hidden_square=32, hidden_hi=32, hidden_lo=32,
)


def head_of(j, kv):
    return 2 * kv + j


def unit(u):
    w = u % 16
    j, kv, qb = w // 8, (w // 4) % 2, w % 4
    if u >= 16:
        return True, j, kv, qb, 0, TOK
    return False, j, kv, qb, max(0, qb - 1), min(TOK, qb + 2)


SIDE = ([("s", 0), ("s", 1)] + [("w", 0, g // 2, g % 2) for g in range(8)] + [("w", 1, g // 2, g % 2) for g in range(8)]
        + [("s", 2)] + [("w", 2, g // 2, g % 2) for g in range(8)] + [("s", 3)])
SIDE_AT = {k: k for k in range(1, 18)}
SIDE_AT.update({k + 2: k for k in range(18, 27)})
TURN_LAG, VALUE_LAG = 2, 3
STAGES = 3
MIX_AT = {8 * (i + 1) + VALUE_LAG: (2 + i // 2, i % 2) for i in range(4)}
STEPS = UNITS + VALUE_LAG + 1


def adds_before(k):
    return sum(s[0] == "w" for s in SIDE[:k])


def sums_before(k):
    return sum(s[0] == "s" for s in SIDE[:k])


def build(nc, x_in, w_in, cols_in, rows_in, row_scale_in, qk_gain_in, rope_in, dist_in, dft_in, head_dft_in, ident_in, out):
    ctx = ExitStack()
    with ctx:
        sems = {}

        def sem(name):
            sems[name] = ctx.enter_context(nc.semaphore(name))
            return sems[name]

        base = (nc.sbuf_base + 31) // 32 * 32
        top = [base]

        def place(name, shape, dt=F32, at=None):
            size = 4 * math.prod(shape[1:])
            offset = top[0] if at is None else at
            t = nc.alloc_sbuf_tensor_at(name, list(shape), dt, offset=offset)
            if at is None:
                top[0] += (size + 31) // 32 * 32
                assert top[0] <= nc.sbuf_usable_end, (name, top[0])
            return t, offset

        x, _ = place("x", [P, TOK, D_MODEL])
        h_hi, at_hi = place("h_hi", [P, KT, SEQ], F32R)
        h_lo, at_lo = place("h_lo", [P, KT, SEQ], F32R)
        mix_hi, _ = place("mix_hi", [P, KT, SEQ], F32R, at=at_hi)
        mix_lo, _ = place("mix_lo", [P, KT, SEQ], F32R, at=at_lo)
        w_raw, _ = place("w_raw", [P, RAW, BLOCK])
        w_hi, _ = place("w_hi", [P, RING, BLOCK], F32R)
        w_lo, _ = place("w_lo", [P, RING, BLOCK], F32R)
        hid_hi, at_hid = place("hid_hi", [P, KT, SEQ], F32R)
        hid_lo, _ = place("hid_lo", [P, KT, SEQ], F32R)
        rest = [at_hid]

        def share(name, shape):
            t, o = place(name, shape, F32, at=rest[0])
            rest[0] += 4 * math.prod(shape[1:])
            assert rest[0] <= at_hid + 2 * 4 * KT * SEQ
            return t

        tk = share("tk", [P, TOK, BANK])
        qkr = share("qkr", [P, TOK, QK])
        dv = share("dv", [P, TOK, P])
        aq = share("aq", [P, 2, SEQ])
        dq = share("dq", [P, 2, SEQ])
        keys = share("keys", [P, 2, SEQ])
        pT = share("pT", [P, 2, BANK])
        y, at_y = place("y", [P, 2, SEQ])
        stage, _ = place("stage", [P, STAGES, BANK])
        bz, _ = place("bz", [P, 2, SEQ])
        bo, _ = place("bo", [P, 2, SEQ])
        co = nc.alloc_sbuf_tensor_at("co", [P, 2, SEQ], F32, offset=at_hid + 4 * TOK * BANK)
        sqg, _ = place("sqg", [P, 2, SEQ], F32, at=at_y)
        sqd, at_sqd = place("sqd", [P, 2, QK])
        rope_a, _ = place("rope_a", [P, QK])
        rope_b, _ = place("rope_b", [P, QK])
        freq, _ = place("freq", [P, 2, BANK], F32, at=at_sqd)
        sine, _ = place("sine", [P, 2, SEQ - HALF], F32, at=at_sqd + 4 * 2 * BANK)
        rows, _ = place("rows", [P, 2 * D_MODEL])
        qk_gain, _ = place("qk_gain", [P, QK])
        cols, _ = place("cols", [P, N_COLS])
        rope, _ = place("rope", [P, 2, TOK, HEAD_DIM])
        dist, _ = place("dist", [P, 3 * P])
        dft, _ = place("dft", [P, TOK, SEQ])
        head_dft, _ = place("head_dft", [P, 2, P])
        ident, _ = place("ident", [P, P])
        ones, _ = place("ones", [P, 1])
        half_neg, _ = place("half_neg", [P, TOK * QK_HEADS])
        row_scale, _ = place("row_scale", [P, 1])
        bn, _ = place("bn", [P, TOK, 2, 6])
        moments, _ = place("moments", [P, TOK, 2])
        var_eps, _ = place("var_eps", [P, TOK])
        rstd, _ = place("rstd", [P, TOK])
        qk_ss, _ = place("qk_ss", [P, TOK, QK_HEADS])
        qk_r, _ = place("qk_r", [P, TOK, QK_HEADS])
        mean_sq, _ = place("mean_sq", [P, 4, TOK])
        group_r, _ = place("group_r", [P, 4, TOK])
        mx, _ = place("mx", [P, 2])
        neg_mx, _ = place("neg_mx", [P, 2])
        p_sum, _ = place("p_sum", [P, 2])
        sink_e, _ = place("sink_e", [P, 2])
        den, _ = place("den", [P, 2])
        inv, _ = place("inv", [P, 2])

        bank = [ctx.enter_context(nc.psum_tensor(f"bank{i}", [P, BANK], F32)) for i in range(8)]

        x_landed = [sem(f"x_landed{t}") for t in range(TOK)]
        w_landed = [sem(f"w_landed{s}") for s in range(RAW)]
        const_landed = sem("const_landed")
        const_set = sem("const_set")
        for name in PER_LAYER:
            sem(name)
        out_written = sem("out_written")

        def at_(l, name, n):
            return l * PER_LAYER[name] + n

        def wait(eng, l, name, n):
            eng.wait_ge(sems[name], at_(l, name, n))

        block = ctx.enter_context(nc.Block())

        @block.sync
        def _(sp):
            for t in range(TOK):
                sp.dma_start(x[:, t, :], x_in[t]).then_inc(x_landed[t], 16)
            for s in range(RAW):
                sp.dma_start(w_raw[:, s, :], w_in[s]).then_inc(w_landed[s], 16)
            with sp.Fori(1, DEPTH * BLOCKS // RAW) as i:
                for s in range(RAW):
                    sp.wait_ge(sems["w_lo"], i * RAW + (s + 1 - RAW))
                    sp.dma_start(w_raw[:, s, :], w_in[bass.ds(i * RAW + s, 1)].rearrange("a p n -> p (a n)")).then_inc(w_landed[s], 16)
            for t in range(TOK):
                sp.wait_ge(sems["scaled"], DEPTH * PER_LAYER["scaled"] + t + 1)
                sp.dma_start(out[t], x[:, t, :]).then_inc(out_written, 16)
            sp.wait_ge(out_written, 16 * TOK)

        @block.tensor
        def _(pe):
            pe.wait_ge(const_landed, 16 * 5)
            pe.wait_ge(const_set, 2)

            def three(dst, s_hi, s_lo, m_hi, m_lo, first, last):
                pe.matmul(dst, s_hi, m_hi, start=first, stop=False)
                pe.matmul(dst, s_hi, m_lo, start=False, stop=False)
                return pe.matmul(dst, s_lo, m_hi, start=False, stop=last)

            def turn(l, which, ct):
                if ct < 4:
                    if which:
                        wait(pe, l, "added", 24 + 4 + ct + 1)
                    else:
                        wait(pe, l, "stats", 8)
                for t in range(TOK):
                    if ct == 0:
                        pe.wait_ge(sems["normed"], 4 * (2 * l + which) + t + 1)
                    last = pe.transpose(bank[4 + ct % 4][:, t * P:(t + 1) * P], x[:, t, ct * P:(ct + 1) * P], ident[:])
                last.then_inc(sems["turned"], 1)

            def turned_products(l, which, product):
                for ct in range(4):
                    turn(l, which, ct)
                for kt in range(KT):
                    wait(pe, l, "h_lo", KT * which + kt + 1)
                    product(kt)
                    if kt + 4 < KT:
                        turn(l, which, kt + 4)

            def w_cols(b, kt, width, c0, n):
                o = kt * width + c0
                return w_hi[:, b % RING, o:o + n], w_lo[:, b % RING, o:o + n]

            def block_ready(l, b):
                wait(pe, l, "w_lo", b + 1)

            with pe.Fori(0, DEPTH) as l:
                def project_d(kt):
                    if kt % 4 == 0:
                        block_ready(l, kt // 4)
                    for t in range(TOK):
                        last = three(bank[t][:], h_hi[:, kt, t * P:(t + 1) * P], h_lo[:, kt, t * P:(t + 1) * P],
                                     *w_cols(kt // 4, kt % 4, BANK, 0, BANK), kt == 0, kt == KT - 1)
                        if kt == KT - 1:
                            last.then_inc(sems["products"], 1)

                turned_products(l, 0, project_d)
                for t in range(TOK):
                    for kt in range(KT):
                        if t == 0 and kt % 4 == 0:
                            block_ready(l, 2 + kt // 4)
                        last = three(bank[4 + t][:], h_hi[:, kt, t * P:(t + 1) * P], h_lo[:, kt, t * P:(t + 1) * P],
                                     *w_cols(2 + kt // 4, kt % 4, BANK, 0, BANK), kt == 0, kt == KT - 1)
                    last.then_inc(sems["products"], 1)
                for m in range(8):
                    b = 4 + m // 2
                    if m % 2 == 0:
                        block_ready(l, b)
                    if m < 4:
                        wait(pe, l, "qk_gain", m + 1)
                        wait(pe, l, "dv_copied", m + 1)
                    else:
                        wait(pe, l, "tk_copied", m - 3)
                    for kt in range(KT):
                        s_hi, s_lo = w_cols(b, kt, 2 * P, (m % 2) * P, P)
                        last = three(bank[m][:], s_hi, s_lo, h_hi[:, kt, :], h_lo[:, kt, :], kt == 0, kt == KT - 1)
                    last.then_inc(sems["products"], 1)
                for ct in range(2):
                    wait(pe, l, "conv_step", 4 * (ct + 1))
                    for t in range(TOK):
                        last = pe.matmul(bank[4 + ct][:], tk[:, t, ct * P:(ct + 1) * P], dft[:, t, :],
                                         start=(t == 0), stop=(t == TOK - 1))
                    last.then_inc(sems["freq"], 1)
                wait(pe, l, "aq_copied", 2)
                wait(pe, l, "bu_copied", 2)
                for j in range(4):
                    for t in range(TOK):
                        if j == 0:
                            wait(pe, l, "qk_roped", t + 1)
                        src = qkr[:, t, j * P:(j + 1) * P] if j < 3 else tk[:, t, 3 * P:4 * P]
                        last = pe.transpose(bank[j][:, t * P:(t + 1) * P], src, ident[:])
                    last.then_inc(sems["qk_turned"], 1)
                for ct in range(2):
                    wait(pe, l, "freq_copied", ct + 1)
                    pe.matmul(bank[4 + ct][:, 0:HALF], head_dft[:, 0, :], freq[:, ct, 0:HALF], start=True, stop=True)
                    pe.matmul(bank[4 + ct][:, HALF:SEQ], head_dft[:, 1, :], freq[:, ct, HALF:SEQ],
                              start=True, stop=True).then_inc(sems["mixed"], 1)

                def side(k):
                    item = SIDE[k]
                    b = bank[6 + k % 2]
                    if k >= 2:
                        if SIDE[k - 2][0] == "s":
                            wait(pe, l, "square_mean", sums_before(k - 2) + 1)
                        else:
                            wait(pe, l, "added", adds_before(k - 2) + 1)
                    if item[0] == "s":
                        g = item[1]
                        wait(pe, l, "group_square", 2 * g + 2)
                        if g == 0:
                            wait(pe, l, "conv_out", 2)
                        for t in range(TOK):
                            for j in range(2):
                                last = pe.matmul(b[:, t:t + 1], sqg[:, j, t * P:(t + 1) * P], ones[:],
                                                 start=(j == 0), stop=(j == 1))
                        last.then_inc(sems["square_sum"], 1)
                    else:
                        output(b, *item[1:])

                def output(dst, g, t, n):
                    if (t, n) == (0, 0):
                        block_ready(l, IN_BLOCKS + g)
                        wait(pe, l, "mix_lo", 2 * g + 2)
                    for j in range(2):
                        c = 2 * g + j
                        last = three(dst[:], mix_hi[:, c, t * P:(t + 1) * P], mix_lo[:, c, t * P:(t + 1) * P],
                                     *w_cols(IN_BLOCKS + g, j, D_MODEL, n * BANK, BANK), j == 0, j == 1)
                    last.then_inc(sems["products"], 1)

                side(0)
                for s in range(STEPS):
                    if s < UNITS:
                        in_d, j, kv, qb, k0, k1 = unit(s)
                        if s == 0:
                            wait(pe, l, "q_copied", 2)
                            wait(pe, l, "k_copied", 2)
                        if s >= 2:
                            wait(pe, l, "probs", s - 1)
                        q = (dq if in_d else aq)[kv * HEAD_DIM:(kv + 1) * HEAD_DIM, j, qb * P:(qb + 1) * P]
                        k = keys[kv * HEAD_DIM:(kv + 1) * HEAD_DIM, 0 if in_d else 1, k0 * P:k1 * P]
                        pe.matmul(bank[s % 2][:, 0:(k1 - k0) * P], q, k, start=True, stop=True).then_inc(sems["scores"], 1)
                    if 0 <= s - TURN_LAG < UNITS:
                        u = s - TURN_LAG
                        _, _, _, _, k0, k1 = unit(u)
                        wait(pe, l, "prob_scaled", u + 1)
                        if u >= 2:
                            wait(pe, l, "prob_copied", u - 1)
                        for i in range(k1 - k0):
                            last = pe.transpose(bank[2 + u % 2][:, i * P:(i + 1) * P], stage[:, u % STAGES, i * P:(i + 1) * P], ident[:])
                        last.then_inc(sems["prob_turned"], 1)
                    if 0 <= s - VALUE_LAG < UNITS:
                        u = s - VALUE_LAG
                        in_d, j, kv, qb, k0, k1 = unit(u)
                        wait(pe, l, "prob_copied", u + 1)
                        if u == 0:
                            wait(pe, l, "fourier_out", 2)
                        if u in (16, 24):
                            wait(pe, l, "mix_lo", 5 + j)
                        for i in range(k1 - k0):
                            v = dv[:, k0 + i, kv * HEAD_DIM:(kv + 1) * HEAD_DIM] if in_d else \
                                tk[:, k0 + i, 2 * P + kv * HEAD_DIM:2 * P + (kv + 1) * HEAD_DIM]
                            last = pe.matmul(bank[4 + j][kv * HEAD_DIM:(kv + 1) * HEAD_DIM, qb * P:(qb + 1) * P], v,
                                             pT[:, u % 2, i * P:(i + 1) * P], start=(i == 0), stop=(i == k1 - k0 - 1))
                        last.then_inc(sems["attended"], 1)
                    if s in SIDE_AT:
                        side(SIDE_AT[s])
                side(len(SIDE) - 1)
                wait(pe, l, "square_mean", 4)
                wait(pe, l, "added", 24)
                for g in range(8):
                    output(bank[g], 3, g // 2, g % 2)

                def hidden(b, m, kt, first, last):
                    s_hi, s_lo = w_cols(b, kt, 2 * P, (m % 2) * P, P)
                    return three(bank[m][:], s_hi, s_lo, h_hi[:, kt, :], h_lo[:, kt, :], first, last)

                def first_hidden(blocks_ready):
                    def product(kt):
                        for m in range(4):
                            if kt == 0 and m % 2 == 0:
                                blocks_ready(m // 2)
                            last = hidden(m // 2, m, kt, kt == 0, kt == KT - 1)
                            if kt == KT - 1:
                                last.then_inc(sems["products"], 1)
                    return product

                def rest_of_chunk(c):
                    def ready(i):
                        pe.wait_ge(sems["w_lo"], l * BLOCKS + c * CHUNK_BLOCKS + (MLP0 + i + 1))
                    for m in range(4, 8):
                        if m % 2 == 0:
                            ready(m // 2)
                        for kt in range(KT):
                            last = hidden(m // 2, m, kt, kt == 0, kt == KT - 1)
                        last.then_inc(sems["products"], 1)
                    for g in range(8):
                        n, t = g // 4, g % 4
                        for kt in range(KT):
                            i = 4 + 2 * n + kt // 4
                            if t == 0 and kt % 4 == 0:
                                ready(i)
                            if g == 0:
                                pe.wait_ge(sems["hidden_lo"], l * 32 + c * KT + (kt + 1))
                            last = three(bank[g][:], hid_hi[:, kt, t * P:(t + 1) * P], hid_lo[:, kt, t * P:(t + 1) * P],
                                         *w_cols(i, kt % 4, BANK, 0, BANK), kt == 0, kt == KT - 1)
                        last.then_inc(sems["products"], 1)

                turned_products(l, 1, first_hidden(lambda i: block_ready(l, MLP0 + i)))
                rest_of_chunk(0)
                with pe.Fori(1, CHUNKS) as c:
                    def ready(i):
                        pe.wait_ge(sems["w_lo"], l * BLOCKS + c * CHUNK_BLOCKS + (MLP0 + i + 1))
                    product = first_hidden(ready)
                    pe.wait_ge(sems["added"], l * PER_LAYER["added"] + c * 8 + (32 - 4))
                    for kt in range(KT):
                        product(kt)
                    pe.wait_ge(sems["added"], l * PER_LAYER["added"] + c * 8 + 32)
                    rest_of_chunk(c)

        @block.scalar
        def _(act):
            act.dma_start(ident[:], ident_in).then_inc(const_landed, 16)
            act.dma_start(rope[:], rope_in).then_inc(const_landed, 16)
            act.dma_start(dist[:], dist_in).then_inc(const_landed, 16)
            act.dma_start(dft[:], dft_in).then_inc(const_landed, 16)
            act.dma_start(head_dft[:], head_dft_in).then_inc(const_landed, 16)

            def split(l, b, released=None):
                act.wait_ge(w_landed[b % RAW], l * (16 * BLOCKS // RAW) + 16 * (b // RAW + 1))
                if released is not None:
                    wait(act, l, "products", released)
                act.copy(w_hi[:, b % RING, :], w_raw[:, b % RAW, :]).then_inc(sems["w_hi"], 1)

            def stream_high(l, which):
                for ct in range(KT):
                    wait(act, l, "y_ready", KT * which + ct + 1)
                    act.copy(h_hi[:, ct, :], y[:, ct % 2, :]).then_inc(sems["h_hi"], 1)

            def split_in_chunk(l, c, i, released):
                b = MLP0 + i
                act.wait_ge(w_landed[b % RAW], l * (16 * BLOCKS // RAW) + c * (16 * CHUNK_BLOCKS // RAW) + 16 * (b // RAW + 1))
                act.wait_ge(sems["products"], l * PER_LAYER["products"] + c * CHUNK_G + (MLP_G0 + released))
                act.copy(w_hi[:, b % RING, :], w_raw[:, b % RAW, :]).then_inc(sems["w_hi"], 1)

            act.wait_ge(const_set, 2)
            split(0, 0)
            split(0, 1)
            with act.Fori(0, DEPTH) as l:
                stream_high(l, 0)
                split(l, 2)
                split(l, 3)
                for t in range(TOK):
                    wait(act, l, "products", t + 1)
                    if t >= 2:
                        wait(act, l, "qk_sum", t - 1)
                    act.activation(sqd[:, t % 2, :], bank[t][:, 0:QK], ACT.Square).then_inc(sems["qk_square"], 1)
                    act.copy(dv[:, t, :], bank[t][:, QK:BANK]).then_inc(sems["dv_copied"], 1)
                split(l, 4, 4)
                split(l, 5, 4)
                for t in range(TOK):
                    wait(act, l, "products", 4 + t + 1)
                    act.copy(tk[:, t, :], bank[4 + t][:]).then_inc(sems["tk_copied"], 1)
                split(l, 6, 8)
                split(l, 7, 8)
                for j in range(2):
                    wait(act, l, "products", 8 + j + 1)
                    act.activation(aq[:, j, :], bank[j][:], ACT.Copy, scale=HEAD_DIM ** -0.5).then_inc(sems["aq_copied"], 1)
                split(l, 8, 10)
                for j in range(2):
                    wait(act, l, "products", 10 + j + 1)
                    act.copy(bz[:, j, :], bank[2 + j][:]).then_inc(sems["bu_copied"], 1)
                split(l, 9, 12)
                split(l, 10, 14)
                split(l, 11, 16)

                def square(j, src):
                    act.activation(sqg[:, j, :], src, ACT.Square).then_inc(sems["group_square"], 1)

                def mix_high(g, j, src):
                    c = 2 * g + j
                    act.activation(mix_hi[:, c, :], src, ACT.Copy, scale=cols[:, COL_GRP + c:COL_GRP + c + 1]).then_inc(sems["mix_hi"], 1)

                for ct in range(2):
                    wait(act, l, "freq", ct + 1)
                    wait(act, l, "qk_roped", TOK)
                    act.copy(freq[:, ct, :], bank[4 + ct][:]).then_inc(sems["freq_copied"], 1)
                for j in range(2):
                    wait(act, l, "conv_out", j + 1)
                    square(j, bo[:, j, :])
                    mix_high(0, j, bo[:, j, :])
                for j in range(2):
                    wait(act, l, "qk_turned", j + 1)
                    act.copy(dq[:, j, :], bank[j][:]).then_inc(sems["q_copied"], 1)
                for ct in range(2):
                    wait(act, l, "mixed", ct + 1)
                    act.copy(sine[:, ct, :], bank[4 + ct][:, HALF:SEQ]).then_inc(sems["sine_copied"], 1)

                for s in range(STEPS):
                    if s < UNITS:
                        in_d, j, kv, qb, k0, k1 = unit(s)
                        n = (k1 - k0) * P
                        if s == 0:
                            for j2 in range(2):
                                wait(act, l, "fourier_out", j2 + 1)
                                wait(act, l, "square_sum", 1)
                                square(j2, co[:, j2, :])
                                mix_high(1, j2, co[:, j2, :])
                        wait(act, l, "neg_max", s + 1)
                        if in_d:
                            wait(act, l, "prob_turned", s - STAGES + 1)
                            act.activation(stage[:, s % STAGES, 0:n], bank[s % 2][:, 0:n], ACT.Exp, bias=neg_mx[:, s % 2:s % 2 + 1],
                                           scale=HEAD_DIM ** -0.5, accum_out=p_sum[:, s % 2:s % 2 + 1]).then_inc(sems["probs"], 1)
                        else:
                            head = head_of(j, kv)
                            act.activation(sink_e[:, s % 2:s % 2 + 1], cols[:, COL_SINK + head:COL_SINK + head + 1], ACT.Exp,
                                           bias=neg_mx[:, s % 2:s % 2 + 1]).then_inc(sems["sink_exp"], 1)
                            act.activation(stage[:, s % STAGES, 0:n], stage[:, s % STAGES, 0:n], ACT.Exp, bias=neg_mx[:, s % 2:s % 2 + 1],
                                           accum_out=p_sum[:, s % 2:s % 2 + 1]).then_inc(sems["probs"], 1)
                    if 0 <= s - TURN_LAG < UNITS:
                        u = s - TURN_LAG
                        _, _, _, _, k0, k1 = unit(u)
                        wait(act, l, "prob_turned", u + 1)
                        if u >= 2:
                            wait(act, l, "attended", u - 1)
                        act.copy(pT[:, u % 2, 0:(k1 - k0) * P], bank[2 + u % 2][:, 0:(k1 - k0) * P]).then_inc(sems["prob_copied"], 1)
                    if s in MIX_AT:
                        g, j = MIX_AT[s]
                        wait(act, l, "attended", 16 * (g - 2) + 8 * (j + 1))
                        wait(act, l, "square_sum", g)
                        square(j, bank[4 + j][:])
                        mix_high(g, j, bank[4 + j][:])
                    if s == 12:
                        split(l, 12, 24)
                    if s == 20:
                        split(l, 13, 32)

                stream_high(l, 1)

                def chunk(c, before_second_half):
                    split_in_chunk(l, c, 2, 0)
                    split_in_chunk(l, c, 3, 0)
                    for m in range(8):
                        act.wait_ge(sems["products"], l * PER_LAYER["products"] + c * CHUNK_G + (MLP_G0 + m + 1))
                        if m >= 2:
                            act.wait_ge(sems["hidden_square"], l * 32 + c * KT + (m - 1))
                            act.wait_ge(sems["hidden_hi"], l * 32 + c * KT + (m - 1))
                        act.activation(stage[:, m % 2, :], bank[m][:], ACT.Relu).then_inc(sems["relu"], 1)
                        act.wait_ge(sems["relu"], l * 32 + c * KT + (m + 1))
                        act.activation(hid_hi[:, m, :], stage[:, m % 2, :], ACT.Square).then_inc(sems["hidden_hi"], 1)
                        if m == 3:
                            split_in_chunk(l, c, 4, 4)
                            split_in_chunk(l, c, 5, 4)
                        if m == 5:
                            split_in_chunk(l, c, 6, 6)
                        if m == 7:
                            split_in_chunk(l, c, 7, 8)
                    before_second_half()

                with act.Fori(0, CHUNKS - 1) as c:
                    def next_chunk():
                        split_in_chunk(l, c, 8, 12)
                        split_in_chunk(l, c, 9, 12)
                    chunk(c, next_chunk)
                chunk(CHUNKS - 1, lambda: None)
                with act.If(l < DEPTH - 1):
                    split(l + 1, 0, 12 - CHUNK_G)
                    split(l + 1, 1, 12 - CHUNK_G)

        @block.vector
        def _(dve):
            dve.memset(ones[:], 1.0).then_inc(const_set, 1)
            dve.memset(half_neg[:], -0.5).then_inc(const_set, 1)
            dve.wait_ge(const_landed, 16 * 5)

            def split(l, b):
                wait(dve, l, "w_hi", b + 1)
                dve.tensor_tensor(w_lo[:, b % RING, :], w_raw[:, b % RAW, :], w_hi[:, b % RING, :].bitcast(F32),
                                  ALU.subtract).then_inc(sems["w_lo"], 1)

            def split_in_chunk(l, c, i):
                b = MLP0 + i
                dve.wait_ge(sems["w_hi"], l * BLOCKS + c * CHUNK_BLOCKS + (b + 1))
                dve.tensor_tensor(w_lo[:, b % RING, :], w_raw[:, b % RAW, :], w_hi[:, b % RING, :].bitcast(F32),
                                  ALU.subtract).then_inc(sems["w_lo"], 1)

            def row_stats(t, n):
                dve.bn_stats(bn[:, t, n, :], x[:, t, n * BANK:(n + 1) * BANK]).then_inc(sems["stats"], 1)

            def variance(k, t, stats_done):
                counted = dve.to_reg(8 * k + stats_done)
                dve.wait_ge(x_landed[t], 16)
                dve.wait_ge(sems["stats"], counted)
                dve.bn_aggr(moments[:, t, :], bn[:, t, :, :].rearrange("p a b -> p (a b)")).then_inc(sems["moments"], 1)
                dve.wait_ge(sems["moments"], 4 * k + (t + 1))
                dve.tensor_scalar(var_eps[:, t:t + 1], moments[:, t, 1:2], LN_EPS, None, ALU.add).then_inc(sems["var_ready"], 1)

            def normalise(k, t):
                dve.wait_ge(sems["rstd"], 4 * k + (t + 1))
                dve.tensor_scalar(x[:, t, :], x[:, t, :], moments[:, t, 0:1], rstd[:, t:t + 1], ALU.subtract, ALU.mult)\
                   .then_inc(sems["normed"], 1)

            def stream_affine(l, which):
                g0, b0 = ((COL_PRE_G, COL_PRE_B), (COL_LN1_G, COL_LN1_B))[which]
                for ct in range(KT):
                    wait(dve, l, "turned", KT * which + ct + 1)
                    if ct >= 2:
                        wait(dve, l, "h_lo", KT * which + ct - 1)
                    dve.tensor_scalar(y[:, ct % 2, :], bank[4 + ct % 4][:], cols[:, g0 + ct:g0 + ct + 1],
                                      cols[:, b0 + ct:b0 + ct + 1], ALU.mult, ALU.add).then_inc(sems["y_ready"], 1)

            for t in range(TOK):
                dve.wait_ge(x_landed[t], 16)
                row_stats(t, 0)
                row_stats(t, 1)
            for t in range(TOK):
                variance(0, t, 2 * t + 2)
            for t in range(TOK):
                normalise(0, t)
            split(0, 0)
            split(0, 1)

            with dve.Fori(0, DEPTH) as l:
                dve.wait_ge(sems["param"], l * 32 + 32)
                stream_affine(l, 0)
                split(l, 2)
                split(l, 3)
                for t in range(TOK):
                    wait(dve, l, "products", t + 1)
                    wait(dve, l, "qk_square", t + 1)
                    wait(dve, l, "dv_copied", t + 1)
                    dve.tensor_tensor(qkr[:, t, :], bank[t][:, 0:QK], qk_gain[:], ALU.mult).then_inc(sems["qk_gain"], 1)
                    dve.tensor_reduce(qk_ss[:, t, :], sqd[:, t % 2, :].rearrange("p (h d) -> p h d", h=QK_HEADS), AX_X, ALU.add)\
                       .then_inc(sems["qk_sum"], 1)
                    wait(dve, l, "qk_sum", t + 1)
                    dve.tensor_scalar(qk_ss[:, t, :], qk_ss[:, t, :], 1.0 / HEAD_DIM, RMS_EPS, ALU.mult, ALU.add)\
                       .then_inc(sems["qk_eps"], 1)
                split(l, 4)
                split(l, 5)
                wait(dve, l, "qk_rstd", 1)
                for t in range(TOK):
                    heads = qkr[:, t, :].rearrange("p (h d) -> p h d", h=QK_HEADS)
                    dve.tensor_tensor(heads, heads, qk_r[:, t, :].unsqueeze(2).to_broadcast([P, QK_HEADS, HEAD_DIM]),
                                      ALU.mult).then_inc(sems["qk_unit"], 1)
                for t in range(TOK):
                    heads = qkr[:, t, :].rearrange("p (h d) -> p h d", h=QK_HEADS)
                    wait(dve, l, "qk_unit", t + 1)
                    if t >= 1:
                        wait(dve, l, "qk_roped", t)
                    dve.tensor_tensor(rope_a[:].rearrange("p (h d) -> p h d", h=QK_HEADS), heads,
                                      rope[:, 0:1, t, :].to_broadcast([P, QK_HEADS, HEAD_DIM]), ALU.mult).then_inc(sems["rope_cos"], 1)
                    m = AXIS_DIM // 2
                    quarters = qkr[:, t, :].rearrange("p (h f m) -> p h f m", h=2 * QK_HEADS, f=2)
                    turned = rope_b[:].rearrange("p (h f m) -> p h f m", h=2 * QK_HEADS, f=2)
                    for f in range(2):
                        sines = rope[:, 1, t, :].rearrange("p (a f m) -> p a f m", a=2, f=2)[:, :, f, :]
                        for_heads = sines.unsqueeze(1).to_broadcast([P, QK_HEADS, 2, m])
                        src = quarters[:, :, 1 - f, :].rearrange("p (h a) m -> p h a m", a=2)
                        dst = turned[:, :, f, :].rearrange("p (h a) m -> p h a m", a=2)
                        dve.tensor_tensor(dst, src, for_heads, ALU.mult).then_inc(sems["rope_sin"], 1)
                    wait(dve, l, "rope_cos", t + 1)
                    wait(dve, l, "rope_sin", 2 * t + 2)
                    dve.tensor_tensor(qkr[:, t, :], rope_a[:], rope_b[:], ALU.add).then_inc(sems["qk_roped"], 1)
                split(l, 6)
                split(l, 7)
                split(l, 8)
                split(l, 9)
                for j in range(2):
                    wait(dve, l, "products", 12 + j + 1)
                    wait(dve, l, "bu_copied", j + 1)
                    z, o = bz[:, j, :], bo[:, j, :]
                    tap = [cols[:, COL_CONV + 2 * i + j:COL_CONV + 2 * i + j + 1] for i in range(3)]
                    dve.tensor_tensor(z, bank[4 + j][:], z, ALU.mult).then_inc(sems["conv_step"], 1)
                    wait(dve, l, "conv_step", 4 * j + 1)
                    dve.tensor_scalar(o, z, tap[1], None, ALU.mult).then_inc(sems["conv_step"], 1)
                    wait(dve, l, "conv_step", 4 * j + 2)
                    dve.scalar_tensor_tensor(out=o[:, 1:SEQ], in0=z[:, 0:SEQ - 1], scalar=tap[0], in1=o[:, 1:SEQ],
                                             op0=ALU.mult, op1=ALU.add).then_inc(sems["conv_step"], 1)
                    wait(dve, l, "conv_step", 4 * j + 3)
                    dve.scalar_tensor_tensor(out=o[:, 0:SEQ - 1], in0=z[:, 1:SEQ], scalar=tap[2], in1=o[:, 0:SEQ - 1],
                                             op0=ALU.mult, op1=ALU.add).then_inc(sems["conv_step"], 1)
                split(l, 10)
                for j in range(2):
                    wait(dve, l, "products", 14 + j + 1)
                    wait(dve, l, "conv_step", 4 * j + 4)
                    dve.tensor_tensor(bo[:, j, :], bank[6 + j][:], bo[:, j, :], ALU.mult).then_inc(sems["conv_out"], 1)
                split(l, 11)

                def mix_low(g, j, src):
                    c = 2 * g + j
                    wait(dve, l, "mix_hi", c + 1)
                    dve.scalar_tensor_tensor(out=mix_lo[:, c, :], in0=src, scalar=cols[:, COL_GRP + c:COL_GRP + c + 1],
                                             in1=mix_hi[:, c, :].bitcast(F32), op0=ALU.mult, op1=ALU.subtract).then_inc(sems["mix_lo"], 1)

                def mean_square(g, k):
                    wait(dve, l, "square_sum", g + 1)
                    dve.tensor_scalar(mean_sq[:, g, :], bank[6 + k % 2][:, 0:TOK], 1.0 / GROUP, RMS_EPS, ALU.mult, ALU.add)\
                       .then_inc(sems["square_mean"], 1)

                def add_output(src, g, t, n, done):
                    wait(dve, l, "products", 16 + 8 * g + 2 * t + n + 1)
                    if (t, n) == (0, 0):
                        wait(dve, l, "group_rstd", g + 1)
                    if g == 0 and n == 0:
                        wait(dve, l, "scaled", t + 1)
                    if g > 0:
                        wait(dve, l, "added", done - 7)
                    xs = x[:, t, n * BANK:(n + 1) * BANK]
                    dve.scalar_tensor_tensor(out=xs, in0=src, scalar=group_r[:, g, t:t + 1], in1=xs, op0=ALU.mult, op1=ALU.add)\
                       .then_inc(sems["added"], 1)

                mix_low(0, 0, bo[:, 0, :])
                mix_low(0, 1, bo[:, 1, :])
                for j in range(2):
                    wait(dve, l, "qk_turned", 3 + j)
                    dve.tensor_copy(keys[:, j, :], bank[2 + j][:]).then_inc(sems["k_copied"], 1)
                mean_square(0, 0)
                for ct in range(2):
                    wait(dve, l, "sine_copied", ct + 1)
                    cosine, o = bank[4 + ct], co[:, ct, :]
                    dve.tensor_tensor(o[:, 1:HALF - 1], cosine[:, 1:HALF - 1], sine[:, ct, :], ALU.subtract).then_inc(sems["fourier_step"], 1)
                    dve.tensor_tensor(o[:, SEQ - 1:HALF - 1:-1], cosine[:, 1:HALF - 1], sine[:, ct, :], ALU.add).then_inc(sems["fourier_step"], 1)
                    dve.tensor_copy(o[:, 0:HALF:HALF - 1], cosine[:, 0:HALF:HALF - 1]).then_inc(sems["fourier_out"], 1)

                def side(k):
                    item = SIDE[k]
                    if item[0] == "s":
                        mean_square(item[1], k)
                    else:
                        add_output(bank[6 + k % 2][:], *item[1:], adds_before(k))

                for s in range(STEPS):
                    if s < UNITS:
                        in_d, j, kv, qb, k0, k1 = unit(s)
                        n = (k1 - k0) * P
                        sl = slice(s % 2, s % 2 + 1)
                        wait(dve, l, "scores", s + 1)
                        if not in_d:
                            head = head_of(j, kv)
                            if s >= STAGES:
                                wait(dve, l, "prob_turned", s - STAGES + 1)
                            d0 = (k0 - qb + 1) * P
                            dve.scalar_tensor_tensor(out=stage[:, s % STAGES, 0:n], in0=dist[:, d0:d0 + n], scalar=2.0 ** (-8.0 * (head + 1) / A_HEADS),
                                                     in1=bank[s % 2][:, 0:n], op0=ALU.mult, op1=ALU.add).then_inc(sems["biased"], 1)
                            wait(dve, l, "biased", s + 1)
                            dve.reduce_max(mx[:, sl], stage[:, s % STAGES, 0:n], AX_X).then_inc(sems["row_max"], 1)
                            wait(dve, l, "row_max", s + 1)
                            dve.tensor_scalar(neg_mx[:, sl], mx[:, sl], cols[:, COL_SINK + head:COL_SINK + head + 1], -1.0,
                                              ALU.max, ALU.mult).then_inc(sems["neg_max"], 1)
                        else:
                            dve.reduce_max(mx[:, sl], bank[s % 2][:, 0:n], AX_X).then_inc(sems["row_max"], 1)
                            wait(dve, l, "row_max", s + 1)
                            dve.tensor_scalar(neg_mx[:, sl], mx[:, sl], -HEAD_DIM ** -0.5, None, ALU.mult).then_inc(sems["neg_max"], 1)
                    if 1 <= s <= UNITS:
                        u = s - 1
                        in_d, _, _, _, k0, k1 = unit(u)
                        sl = slice(u % 2, u % 2 + 1)
                        wait(dve, l, "probs", u + 1)
                        total = p_sum[:, sl]
                        if not in_d:
                            dve.tensor_tensor(den[:, sl], p_sum[:, sl], sink_e[:, sl], ALU.add).then_inc(sems["denom"], 1)
                            wait(dve, l, "denom", u + 1)
                            total = den[:, sl]
                        dve.reciprocal(inv[:, sl], total).then_inc(sems["inv_denom"], 1)
                        wait(dve, l, "inv_denom", u + 1)
                        p = stage[:, u % STAGES, 0:(k1 - k0) * P]
                        dve.tensor_scalar(p, p, inv[:, sl], None, ALU.mult).then_inc(sems["prob_scaled"], 1)
                    if s in SIDE_AT:
                        side(SIDE_AT[s])
                    if s == 0:
                        mix_low(1, 0, co[:, 0, :])
                        mix_low(1, 1, co[:, 1, :])
                    if s in MIX_AT:
                        mix_low(*MIX_AT[s], bank[4 + MIX_AT[s][1]][:])
                    if s == 12:
                        split(l, 12)
                    if s == 20:
                        split(l, 13)
                side(len(SIDE) - 1)
                k = 2 * l + 1
                for t in range(TOK):
                    for n in range(2):
                        add_output(bank[2 * t + n][:], 3, t, n, 24 + 2 * t + n)
                        wait(dve, l, "added", 24 + 2 * t + n + 1)
                        row_stats(t, n)
                    variance(k, t, 2 * t + 2)
                    if t >= 1:
                        normalise(k, t - 1)
                normalise(k, TOK - 1)
                stream_affine(l, 1)

                def chunk(c, last):
                    split_in_chunk(l, c, 2)
                    split_in_chunk(l, c, 3)
                    for m in range(9):
                        if m < 8:
                            dve.wait_ge(sems["relu"], l * 32 + c * KT + (m + 1))
                            if m >= 2:
                                dve.wait_ge(sems["hidden_lo"], l * 32 + c * KT + (m - 1))
                            r = stage[:, m % 2, :]
                            dve.tensor_tensor(y[:, m % 2, :], r, r, ALU.mult).then_inc(sems["hidden_square"], 1)
                        if m >= 1:
                            i = m - 1
                            dve.wait_ge(sems["hidden_hi"], l * 32 + c * KT + (i + 1))
                            dve.wait_ge(sems["hidden_square"], l * 32 + c * KT + (i + 1))
                            dve.tensor_tensor(hid_lo[:, i, :], y[:, i % 2, :], hid_hi[:, i, :].bitcast(F32), ALU.subtract)\
                               .then_inc(sems["hidden_lo"], 1)
                        if m == 4:
                            split_in_chunk(l, c, 4)
                            split_in_chunk(l, c, 5)
                        if m == 6:
                            split_in_chunk(l, c, 6)
                        if m == 8:
                            split_in_chunk(l, c, 7)
                    for g in range(8):
                        n, t = g // 4, g % 4
                        dve.wait_ge(sems["products"], l * PER_LAYER["products"] + c * CHUNK_G + (MLP_G0 + 8 + g + 1))
                        if g == 0:
                            dve.wait_ge(sems["scaled"], l * 8 + 8)
                            dve.wait_ge(sems["added"], l * PER_LAYER["added"] + c * 8 + 32)
                        xs = x[:, t, n * BANK:(n + 1) * BANK]
                        dve.tensor_tensor(xs, bank[g][:], xs, ALU.add).then_inc(sems["added"], 1)
                        if g == 3 and not last:
                            split_in_chunk(l, c, 8)
                            split_in_chunk(l, c, 9)
                        if last and g == 3:
                            with dve.If(l < DEPTH - 1):
                                split(l + 1, 0)
                                split(l + 1, 1)
                        if last:
                            wait(dve, l, "added", 32 + 8 * (CHUNKS - 1) + g + 1)
                            row_stats(t, n)
                            if n == 1:
                                variance(2 * l + 2, t, 4 + t + 1)
                                normalise(2 * l + 2, t)

                with dve.Fori(0, CHUNKS - 1) as c:
                    chunk(c, False)
                chunk(CHUNKS - 1, True)

        @block.gpsimd
        def _(pool):
            def load_params(l):
                pool.dma_start(cols[:], cols_in[bass.ds(l, 1)].rearrange("a p n -> p (a n)")).then_inc(sems["param"], 16)
                pool.dma_start(qk_gain[:], qk_gain_in[bass.ds(l, 1)].to_broadcast([P, QK])).then_inc(sems["param"], 16)

            def load_rows(k):
                pool.dma_start(rows[:], rows_in[bass.ds(k, 1)].to_broadcast([P, 2 * D_MODEL])).then_inc(sems["rows"], 16)
                pool.dma_start(row_scale[:], row_scale_in[bass.ds(k, 1)].to_broadcast([P, 1])).then_inc(sems["rows"], 16)

            def scale_rows(k):
                counted = pool.to_reg(k * 32 + 32)
                pool.wait_ge(const_set, 2)
                pool.wait_ge(sems["rows"], counted)
                pool.tensor_scalar(rows[:], rows[:], row_scale[:], None, ALU.mult).then_inc(sems["row_ready"], 1)

            def power(dst, src, n):
                return pool.tensor_tensor(dst, src, half_neg[:, 0:n], ALU.pow)

            def layer_norm_rstd(k):
                for t in range(TOK):
                    pool.wait_ge(sems["var_ready"], 4 * k + (t + 1))
                    power(rstd[:, t:t + 1], var_eps[:, t:t + 1], 1).then_inc(sems["rstd"], 1)

            def stream_low(l, which):
                for ct in range(KT):
                    wait(pool, l, "h_hi", KT * which + ct + 1)
                    pool.tensor_tensor(h_lo[:, ct, :], y[:, ct % 2, :], h_hi[:, ct, :].bitcast(F32), ALU.subtract).then_inc(sems["h_lo"], 1)

            def residual(k, scaled_before):
                pool.wait_ge(sems["row_ready"], k + 1)
                for t in range(TOK):
                    pool.tensor_tensor(x[:, t, :], x[:, t, :], rows[:, 0:D_MODEL], ALU.mult).then_inc(sems["gained"], 1)
                for t in range(TOK):
                    pool.wait_ge(sems["gained"], scaled_before + t + 1)
                    pool.tensor_tensor(x[:, t, :], x[:, t, :], rows[:, D_MODEL:], ALU.add).then_inc(sems["scaled"], 1)

            load_params(0)
            load_rows(0)
            layer_norm_rstd(0)
            scale_rows(0)
            with pool.Fori(0, DEPTH) as l:
                stream_low(l, 0)
                wait(pool, l, "turned", KT)
                residual(2 * l, l * 8)
                pool.wait_ge(sems["scaled"], l * 8 + 4)
                load_rows(2 * l + 1)
                scale_rows(2 * l + 1)
                wait(pool, l, "qk_eps", TOK)
                power(qk_r[:].rearrange("p t h -> p (t h)"), qk_ss[:].rearrange("p t h -> p (t h)"), TOK * QK_HEADS)\
                    .then_inc(sems["qk_rstd"], 1)
                for g in range(4):
                    wait(pool, l, "square_mean", g + 1)
                    power(group_r[:, g, :], mean_sq[:, g, :], TOK).then_inc(sems["group_rstd"], 1)
                layer_norm_rstd(2 * l + 1)
                stream_low(l, 1)
                wait(pool, l, "turned", 2 * KT)
                residual(2 * l + 1, l * 8 + 4)
                pool.wait_ge(sems["scaled"], l * 8 + 8)
                load_params(l + 1)
                load_rows(2 * l + 2)
                scale_rows(2 * l + 2)
                layer_norm_rstd(2 * l + 2)
            pool.wait_ge(sems["normed"], 4 * (2 * DEPTH + 1))
            residual(2 * DEPTH, 8 * DEPTH)


def lay_out(x, ln_in_g, ln_in_b, w_in, conv_w, sink, qn_g, kn_g, grp_g, w_out, ln1_g, ln1_b, w1, w2, ln2_g, ln2_b):
    a = {k: np.asarray(v) for k, v in dict(
        x=x, ln_in_g=ln_in_g, ln_in_b=ln_in_b, w_in=w_in, conv_w=conv_w, sink=sink, qn_g=qn_g, kn_g=kn_g, grp_g=grp_g,
        w_out=w_out, ln1_g=ln1_g, ln1_b=ln1_b, w1=w1, w2=w2, ln2_g=ln2_g, ln2_b=ln2_b).items()}
    lane = np.arange(HEAD_DIM)
    heads = np.concatenate([head_of(j, kv) * HEAD_DIM + lane for j in range(2) for kv in range(2)])
    order = dict(a_q=0, a_k=256, a_v=384, b_u=512, b_gate=768, c_gate=1024, c_u=1280, d_q=1536, d_k=1792, d_v=1920)

    def columns(name, n, perm=None):
        return order[name] + (np.arange(n) if perm is None else perm)

    def tiles(w, n_rows, width):
        return w.reshape(n_rows, P, width).transpose(1, 0, 2).reshape(P, n_rows * width)

    weights = np.empty((DEPTH * BLOCKS, P, BLOCK), np.float32)
    cols = np.empty((DEPTH + 1, P, N_COLS), np.float32)
    for l in range(DEPTH + 1):
        m = min(l, DEPTH - 1)
        pre = (a["ln_in_g"], a["ln_in_b"]) if l == 0 else (a["ln2_g"][l - 1], a["ln2_b"][l - 1])
        grp = a["grp_g"][m].reshape(4, GROUP)
        groups = [grp[1], grp[2], grp[0][heads], grp[3][heads]]
        for c, v in ((COL_PRE_G, pre[0]), (COL_PRE_B, pre[1]), (COL_LN1_G, a["ln1_g"][m]), (COL_LN1_B, a["ln1_b"][m]),
                     (COL_CONV, a["conv_w"][m].reshape(-1)), (COL_GRP, np.concatenate(groups))):
            cols[l, :, c:c + v.size // P] = v.reshape(-1, P).T
        cols[l, :, COL_SINK:] = a["sink"][m][None, :]
    for l in range(DEPTH):
        blocks = weights[l * BLOCKS:(l + 1) * BLOCKS]
        w = a["w_in"][l]
        token_major = [np.concatenate([columns("d_q", 256, heads), columns("d_k", P), columns("d_v", P)]),
                       np.concatenate([columns("c_u", 256), columns("a_v", P), columns("a_k", P)])]
        for i, c in enumerate(token_major):
            for j in range(2):
                blocks[2 * i + j] = tiles(w[j * 512:(j + 1) * 512, c], 4, BANK)
        channel_major = [columns("a_q", 256, heads), columns("b_u", 256), columns("c_gate", 256), columns("b_gate", 256)]
        for i, c in enumerate(channel_major):
            blocks[4 + i] = tiles(w[:, c], KT, 2 * P)
        wo = a["w_out"][l].reshape(4, GROUP, D_MODEL)
        for i, g in enumerate([wo[1], wo[2], wo[0][heads], wo[3][heads]]):
            blocks[IN_BLOCKS + i] = tiles(g, 2, D_MODEL)
        for c in range(CHUNKS):
            first = MLP0 + c * CHUNK_BLOCKS
            for i in range(4):
                lo = c * 1024 + i * 256
                blocks[first + i] = tiles(a["w1"][l][:, lo:lo + 256], KT, 256)
            for i in range(4):
                n, k = i // 2, i % 2
                lo = c * 1024 + k * 512
                blocks[first + 4 + i] = tiles(a["w2"][l][lo:lo + 512, n * BANK:(n + 1) * BANK], 4, BANK)
    rows = np.stack([np.concatenate([a["ln_in_g"], a["ln_in_b"]])]
                    + [np.concatenate([a[f"{n}_g"][l], a[f"{n}_b"][l]]) for l in range(DEPTH) for n in ("ln1", "ln2")])
    qk_gain = np.stack([np.concatenate([np.tile(a["qn_g"][l], 4), np.tile(a["kn_g"][l], 2)])
                        for l in list(range(DEPTH)) + [DEPTH - 1]])
    f32 = np.float32
    row_scale = np.full((2 * DEPTH + 1, 1), ALPHA, f32)
    row_scale[-1] = 1.0
    inv_freq = (f32(ROPE_THETA) ** (-np.arange(0, AXIS_DIM, 2, dtype=f32) / f32(AXIS_DIM))).astype(f32)
    tok = np.arange(SEQ)
    angle = np.stack([(tok // GRID_W).astype(f32)[:, None] * inv_freq, (tok % GRID_W).astype(f32)[:, None] * inv_freq], 1)
    angle = angle.astype(np.float64)
    cosine = np.stack([np.cos(angle), np.cos(angle)], 2).reshape(SEQ, HEAD_DIM)
    sine = np.stack([-np.sin(angle), np.sin(angle)], 2).reshape(SEQ, HEAD_DIM)
    rope = np.stack([cosine, sine]).reshape(2, TOK, P, HEAD_DIM).transpose(2, 0, 1, 3).astype(f32)
    gap = np.abs(np.arange(P)[:, None] + P - np.arange(3 * P)[None, :])
    dist = np.where(gap <= WINDOW, -gap, -1e33).astype(f32)
    turn = 2 * np.pi * (np.outer(tok, tok) % SEQ) / SEQ
    dft = np.concatenate([np.cos(turn[:, :HALF]), np.sin(turn[:, 1:HALF - 1])], 1) / np.sqrt(SEQ)
    dft = dft.reshape(TOK, P, SEQ).transpose(1, 0, 2).astype(f32)
    turn = 2 * np.pi * (np.outer(lane, lane) % HEAD_DIM) / HEAD_DIM
    head_dft = np.zeros((P, 2, P))
    for h in range(2):
        sl = slice(h * HEAD_DIM, (h + 1) * HEAD_DIM)
        head_dft[sl, 0, sl] = np.cos(turn) / np.sqrt(HEAD_DIM)
        head_dft[sl, 1, sl] = np.sin(turn) / np.sqrt(HEAD_DIM)
    return dict(x=a["x"].reshape(TOK, P, D_MODEL), weights=weights, cols=cols, rows=rows, row_scale=row_scale,
                qk_gain=qk_gain, rope=np.ascontiguousarray(rope), dist=dist, dft=np.ascontiguousarray(dft),
                head_dft=head_dft.astype(f32), ident=np.eye(P, dtype=f32))


def kernel(**inputs):
    import concourse.bacc as bacc
    from concourse.bass_utils import run_bass_kernel_spmd

    nc = bacc.Bacc("TRN2", target_bir_lowering=False, num_devices=1)
    arrays, args = {}, []
    for name, array in lay_out(**inputs).items():
        arrays[f"in_{name}"] = np.ascontiguousarray(array)
        args.append(nc.dram_tensor(f"in_{name}", array.shape, mybir.dt.from_np(array.dtype), kind="ExternalInput").ap())
    out = nc.dram_tensor("out_h", (TOK, P, D_MODEL), F32, kind="ExternalOutput").ap()
    build(nc, *args, out)
    result = run_bass_kernel_spmd(nc, [arrays], core_ids=[0])
    return result.results[0]["out_h"].reshape(1, SEQ, D_MODEL)
```

```python
import math
from contextlib import ExitStack

import numpy as np

import concourse.bass as bass
from concourse import mybir

F32 = mybir.dt.float32
F32R = mybir.dt.float32r
ALU = mybir.AluOpType
ACT = mybir.ActivationFunctionType
AX_X = mybir.AxisListType.X

P = 128
D_MODEL = 1024
SEQ = 512
DEPTH = 2
HEAD_DIM = 64
GROUP = 256
D_FF = 4 * D_MODEL
WINDOW = 128
GRID_W = 64
AXIS_DIM = HEAD_DIM // 2
ROPE_THETA = 10000.0
LN_EPS = 1e-5
RMS_EPS = 1e-6
ALPHA = (2 * DEPTH) ** 0.25
A_HEADS = 4

TOK = SEQ // P
KT = D_MODEL // P
BANK = 512
BLOCK = 2048
RAW = 2
RING = 4
IN_BLOCKS = 2 * D_MODEL // (BLOCK // KT)
OUT_BLOCKS = 4
CHUNKS = D_FF // D_MODEL
CHUNK_BLOCKS = 8
MLP0 = IN_BLOCKS + OUT_BLOCKS
BLOCKS = MLP0 + CHUNKS * CHUNK_BLOCKS
MLP_G0 = 48
CHUNK_G = 16
QK = GROUP + P
QK_HEADS = QK // HEAD_DIM
UNITS = 32
HALF = SEQ // 2 + 1

COL_CONV, COL_GRP, COL_SINK = 0, 6, 10
N_COLS = 14

PER_LAYER = dict(
    w_hi=BLOCKS, w_lo=BLOCKS, products=MLP_G0 + CHUNKS * CHUNK_G,
    turned=4 * TOK, h_hi=4 * TOK, h_lo=4 * TOK,
    stats=16, moments=8, var_ready=8, rstd=8, centred=8, normed=16, rows=32,
    param=32, head_gain=16,
    qk_gain=TOK, qk_square=TOK, dv_copied=TOK, qk_sum=TOK, qk_eps=TOK, qk_rstd=1, qk_unit=TOK,
    rope_cos=TOK, rope_sin=2 * TOK, qk_roped=TOK, tk_copied=TOK, aq_hi=2, aq_lo=2, bu_copied=2,
    conv_step=8, conv_out=2, group_square=4, square_added=2, square_sum=2,
    mix_hi=12, mix_lo=12, square_mean=10, group_rstd=10,
    qk_turned=4, k_hi=2, k_lo=2, dq_copied=2, dq_hi=2, dq_lo=2, freq=2, freq_copied=2, mixed=2, sine_copied=2, fourier_step=4, fourier_out=2,
    scores=UNITS, biased=16, row_max=UNITS, neg_max=UNITS, sink_exp=16, probs=UNITS, denom=4,
    inv_denom=8, head_out=8, out_square=8, out_gained=8, mix_turned=8, prob_turned=UNITS, prob_copied=UNITS, attended=UNITS,
    added=4 * 8 + CHUNKS * 8, relu=32, hidden_square=32, hidden_hi=32, hidden_lo=32,
)


def head_of(j, kv):
    return 2 * kv + j


def unit(u):
    qb, j, kv = (u % 16) // 4, (u // 2) % 2, u % 2
    if u >= 16:
        return True, j, kv, qb, 0, TOK
    return False, j, kv, qb, max(0, qb - 1), min(TOK, qb + 2)


STAGES = 3
TURN_LAG, VALUE_LAG = 1, 1
STEPS = UNITS + VALUE_LAG


def quad_scaled_in(step):
    q, rest = divmod(step - VALUE_LAG - 3, 4)
    return q if rest == 0 and q >= 0 else None


def quad_turned_in(step):
    return quad_scaled_in(step - 1)


def w_items(g, t0=0, t1=TOK):
    return [("w", g, t, n) for t in range(t0, t1) for n in range(2)]


SIDE_STEPS = {-1: [("s", 0)], 0: w_items(0, 0, 1), 4: [("s", 1)],
              27: [("t", 0, 0), ("t", 0, 1)], 32: [("t", 1, 0), ("t", 1, 1)]}
SIDE_STEPS.update(zip((1, 2, 3, 5, 6, 7), ([item] for item in w_items(0, 1))))
SIDE_STEPS.update(zip(range(8, 16), ([item] for item in w_items(1))))
SIDE_STEPS.update(zip((16, 17, 18, 19, 20, 21, 25, 29), ([item] for item in w_items(2))))
SIDE_STEPS.update(zip((22, 23, 26, 28, 30, 31), ([item] for item in w_items(3, 0, 3))))
SIDE = sum((SIDE_STEPS[_step] for _step in sorted(SIDE_STEPS)), [])
FIRST_OF = {}
for _step in sorted(SIDE_STEPS):
    FIRST_OF[_step] = sum(len(SIDE_STEPS[_s]) for _s in SIDE_STEPS if _s < _step)
TAIL = len(SIDE)
SIDE += w_items(3, 3, 4) + [("t", t, half) for t in (2, 3) for half in range(2)]
NORM_AT = {24: 0, 28: 1}


def sides_of(step):
    return range(FIRST_OF[step], FIRST_OF[step] + len(SIDE_STEPS[step])) if step in SIDE_STEPS else ()


def kind_before(k, kind):
    return sum(s[0] == kind for s in SIDE[:k])


def adds_before(k):
    return kind_before(k, "w")


def last_add(k):
    return max([adds_before(i) + 1 for i in range(k) if SIDE[i][0] == "w" and SIDE[i][2:] == SIDE[k][2:]], default=0)


def build(nc, x_in, w_in, cols_in, rows_in, qk_gain_in, head_gain_in, rope_in, dist_in, dft_in, head_dft_in, ident_in, out):
    ctx = ExitStack()
    with ctx:
        sems = {}

        def sem(name):
            sems[name] = ctx.enter_context(nc.semaphore(name))
            return sems[name]

        base = (nc.sbuf_base + 31) // 32 * 32
        top = [base]

        def place(name, shape, dt=F32, at=None):
            size = 4 * math.prod(shape[1:])
            offset = top[0] if at is None else at
            t = nc.alloc_sbuf_tensor_at(name, list(shape), dt, offset=offset)
            if at is None:
                top[0] += (size + 31) // 32 * 32
                assert top[0] <= nc.sbuf_usable_end, (name, top[0])
            return t, offset

        x, _ = place("x", [P, TOK, D_MODEL])
        h_hi, at_hi = place("h_hi", [P, KT, SEQ], F32R)
        h_lo, at_lo = place("h_lo", [P, KT, SEQ], F32R)
        mix_hi, _ = place("mix_hi", [P, KT, SEQ], F32R, at=at_hi)
        mix_lo, _ = place("mix_lo", [P, KT, SEQ], F32R, at=at_lo)
        w_raw, _ = place("w_raw", [P, RAW, BLOCK])
        w_hi, _ = place("w_hi", [P, RING, BLOCK], F32R)
        w_lo, _ = place("w_lo", [P, RING, BLOCK], F32R)
        hid_hi, at_hid = place("hid_hi", [P, KT, SEQ], F32R)
        hid_lo, _ = place("hid_lo", [P, KT, SEQ], F32R)
        rest = [at_hid]

        def share(name, shape, dt=F32):
            t, _ = place(name, shape, dt, at=rest[0])
            rest[0] += 4 * math.prod(shape[1:])
            assert rest[0] <= at_hid + 2 * 4 * KT * SEQ
            return t

        tk = share("tk", [P, TOK, BANK])
        qkr = share("qkr", [P, TOK, QK])
        dv = share("dv", [P, TOK, P])
        aq_lo = share("aq_lo", [P, 2, SEQ], F32R)
        dq = share("dq", [P, 2, SEQ])
        dq_lo, _ = place("dq_lo", [P, 2, SEQ], F32R, at=rest[0] - 4 * 2 * SEQ)
        keys_lo = share("keys_lo", [P, 2, SEQ], F32R)
        pT = share("pT", [P, 2, BANK])
        y, at_y = place("y", [P, 2, SEQ])
        stage, _ = place("stage", [P, STAGES, BANK])
        bz, at_bz = place("bz", [P, 2, SEQ])
        head_out, _ = place("head_out", [P, 2, GROUP], F32, at=at_bz)
        head_gain, _ = place("head_gain", [P, 2, GROUP], F32, at=at_bz + 4 * 2 * GROUP)
        head_gained, _ = place("head_gained", [P, 2, GROUP], F32, at=at_y)
        bo, at_bo = place("bo", [P, 2, SEQ])
        dq_hi, _ = place("dq_hi", [P, 2, SEQ], F32R, at=at_bo)
        dk_hi, _ = place("dk_hi", [P, SEQ], F32R, at=at_hid + 4 * (TOK * BANK + 2 * SEQ))
        co = nc.alloc_sbuf_tensor_at("co", [P, 2, SEQ], F32, offset=at_hid + 4 * TOK * BANK)
        sqg, _ = place("sqg", [P, 2, SEQ], F32, at=at_y)
        sqd, at_sqd = place("sqd", [P, 2, QK])
        rope_a, _ = place("rope_a", [P, QK])
        rope_b, _ = place("rope_b", [P, QK])
        freq, _ = place("freq", [P, 2, BANK], F32, at=at_sqd)
        head_square, _ = place("head_square", [P, GROUP], F32, at=at_sqd)
        sine, _ = place("sine", [P, 2, SEQ - HALF], F32, at=at_sqd + 4 * 2 * BANK)
        rows, at_rows = place("rows", [P, 2 * D_MODEL])
        aq_hi, _ = place("aq_hi", [P, 2, SEQ], F32R, at=at_rows)
        ak_hi, _ = place("ak_hi", [P, SEQ], F32R, at=at_rows + 4 * 2 * SEQ)
        qk_gain, _ = place("qk_gain", [P, QK])
        cols, _ = place("cols", [P, N_COLS])
        rope, _ = place("rope", [P, 2, TOK, HEAD_DIM])
        dist, _ = place("dist", [P, 3 * P])
        dft, _ = place("dft", [P, TOK, SEQ])
        head_dft, _ = place("head_dft", [P, 2, P])
        ident, _ = place("ident", [P, P])
        ones, _ = place("ones", [P, 1])
        half_neg, _ = place("half_neg", [P, TOK * QK_HEADS])
        bn, _ = place("bn", [P, TOK, 2, 6])
        moments, _ = place("moments", [P, TOK, 2])
        var_eps, _ = place("var_eps", [P, TOK])
        rstd, _ = place("rstd", [P, TOK])
        qk_ss, _ = place("qk_ss", [P, TOK, QK_HEADS])
        qk_r, _ = place("qk_r", [P, TOK, QK_HEADS])
        mean_sq, _ = place("mean_sq", [P, 4, TOK])
        group_r, _ = place("group_r", [P, 4, TOK])
        mx, _ = place("mx", [P, 2])
        neg_mx, _ = place("neg_mx", [P, 2])
        p_sum, _ = place("p_sum", [P, 2, 4])
        sink_e, _ = place("sink_e", [P, 2, 4])
        den, _ = place("den", [P, 2, 4])
        inv, _ = place("inv", [P, 2, 4])
        head_ss, _ = place("head_ss", [P, 2])

        bank = [ctx.enter_context(nc.psum_tensor(f"bank{i}", [P, BANK], F32)) for i in range(8)]

        x_landed = [sem(f"x_landed{t}") for t in range(TOK)]
        w_landed = [sem(f"w_landed{s}") for s in range(RAW)]
        ident_landed = sem("ident_landed")
        const_landed = sem("const_landed")
        sem("table")
        const_set = sem("const_set")
        for name in PER_LAYER:
            sem(name)
        out_written = sem("out_written")

        def at_(l, name, n):
            return l * PER_LAYER[name] + n

        def wait(eng, l, name, n):
            eng.wait_ge(sems[name], at_(l, name, n))

        def turn_bank(which, t, half):
            return bank[6 + SIDE.index(("t", t, half)) % 2 if which else 4 + 2 * (t % 2) + half]

        def turned_half(which, t, half):
            place_in_h = (slice(None), slice(4 * half, 4 * half + 4), slice(t * P, (t + 1) * P))
            return turn_bank(which, t, half)[:].rearrange("p (c n) -> p c n", c=4), place_in_h

        def turned_quad(q):
            src = bank[4 + q % 2][:, GROUP:].rearrange("p (c n) -> p c n", c=2)
            g, t = 2 + q // 4, q % 4
            return src, (slice(None), slice(2 * g, 2 * g + 2), slice(t * P, (t + 1) * P))

        def chunk_bank(g, last):
            return bank[(g + 4) % 8 if last else g]

        block = ctx.enter_context(nc.Block())

        @block.sync
        def _(sp):
            def load_weights(b):
                sp.dma_start(w_raw[:, b, :], w_in[b]).then_inc(w_landed[b], 16)

            def load_tile(t):
                sp.dma_start(x[:, t, :], x_in[t]).then_inc(x_landed[t], 16)

            load_tile(0)
            load_weights(0)
            sp.wait_ge(x_landed[0], 16)
            load_tile(1)
            load_weights(1)
            load_tile(2)
            load_tile(3)
            sp.dma_start(rope[:], rope_in).then_inc(const_landed, 16)
            sp.dma_start(dist[:], dist_in).then_inc(const_landed, 16)
            sp.dma_start(dft[:], dft_in).then_inc(const_landed, 16)
            sp.dma_start(head_dft[:], head_dft_in).then_inc(const_landed, 16)
            with sp.Fori(1, DEPTH * BLOCKS // RAW) as i:
                for s in range(RAW):
                    sp.wait_ge(sems["w_lo"], i * RAW + (s + 1 - RAW))
                    sp.dma_start(w_raw[:, s, :], w_in[bass.ds(i * RAW + s, 1)].rearrange("a p n -> p (a n)")).then_inc(w_landed[s], 16)
            for t in range(TOK):
                for half in range(2):
                    sp.wait_ge(sems["normed"], DEPTH * PER_LAYER["normed"] + 2 * t + half + 1)
                    c = slice(half * BANK, (half + 1) * BANK)
                    sp.dma_start(out[t, :, c], x[:, t, c]).then_inc(out_written, 16)
            sp.wait_ge(out_written, 2 * 16 * TOK)

        @block.tensor
        def _(pe):
            pe.wait_ge(ident_landed, 16)
            pe.wait_ge(const_set, 2)

            def three(dst, s_hi, s_lo, m_hi, m_lo, first, last):
                pe.matmul(dst, s_hi, m_hi, start=first, stop=False)
                pe.matmul(dst, s_hi, m_lo, start=False, stop=False)
                return pe.matmul(dst, s_lo, m_hi, start=False, stop=last)

            def turn_half(l, which, t, half):
                wait(pe, l, "normed", 2 * TOK * which + 2 * t + half + 1)
                for c in range(4):
                    ct = 4 * half + c
                    last = pe.transpose(turn_bank(which, t, half)[:, c * P:(c + 1) * P], x[:, t, ct * P:(ct + 1) * P], ident[:])
                last.then_inc(sems["turned"], 1)

            def turn(l, t):
                if t >= 2:
                    wait(pe, l, "h_lo", 2 * (t - 2) + 2)
                turn_half(l, 0, t, 0)
                turn_half(l, 0, t, 1)

            def w_cols(b, kt, width, c0, n):
                o = kt * width + c0
                return w_hi[:, b % RING, o:o + n], w_lo[:, b % RING, o:o + n]

            def block_ready(l, b):
                wait(pe, l, "w_lo", b + 1)

            def keep_warm(n):
                for _ in range(n):
                    pe.transpose(bank[0][:, 0:P], ident[:], ident[:])

            keep_warm(40)
            turn(0, 0)
            keep_warm(24)
            with pe.Fori(0, DEPTH) as l:
                for t in range(TOK):
                    for kt in range(KT):
                        if kt == KT // 2 and t + 1 < TOK:
                            turn(l, t + 1)
                        if kt % 4 == 0:
                            wait(pe, l, "h_lo", 2 * t + kt // 4 + 1)
                            if t == 0:
                                block_ready(l, kt // 4)
                        last = three(bank[t][:], h_hi[:, kt, t * P:(t + 1) * P], h_lo[:, kt, t * P:(t + 1) * P],
                                     *w_cols(kt // 4, kt % 4, BANK, 0, BANK), kt == 0, kt == KT - 1)
                    last.then_inc(sems["products"], 1)
                for t in range(TOK):
                    for kt in range(KT):
                        if t == 0 and kt % 4 == 0:
                            block_ready(l, 2 + kt // 4)
                        last = three(bank[4 + t][:], h_hi[:, kt, t * P:(t + 1) * P], h_lo[:, kt, t * P:(t + 1) * P],
                                     *w_cols(2 + kt // 4, kt % 4, BANK, 0, BANK), kt == 0, kt == KT - 1)
                    last.then_inc(sems["products"], 1)
                for m in range(8):
                    b = 4 + m // 2
                    if m % 2 == 0:
                        block_ready(l, b)
                    if m < 4:
                        wait(pe, l, "qk_gain", m + 1)
                        wait(pe, l, "dv_copied", m + 1)
                    else:
                        wait(pe, l, "tk_copied", m - 3)
                    for kt in range(KT):
                        s_hi, s_lo = w_cols(b, kt, 2 * P, (m % 2) * P, P)
                        last = three(bank[m][:], s_hi, s_lo, h_hi[:, kt, :], h_lo[:, kt, :], kt == 0, kt == KT - 1)
                    last.then_inc(sems["products"], 1)
                wait(pe, l, "aq_lo", 2)
                wait(pe, l, "bu_copied", 2)
                for j in range(4):
                    for t in range(TOK):
                        if j == 0:
                            wait(pe, l, "qk_roped", t + 1)
                        src = qkr[:, t, j * P:(j + 1) * P] if j < 3 else tk[:, t, 3 * P:4 * P]
                        last = pe.transpose(bank[j][:, t * P:(t + 1) * P], src, ident[:])
                    last.then_inc(sems["qk_turned"], 1)
                pe.wait_ge(const_landed, 16 * 4)
                for ct in range(2):
                    wait(pe, l, "conv_step", 4 * (ct + 1))
                    for t in range(TOK):
                        last = pe.matmul(bank[4 + ct][:], tk[:, t, ct * P:(ct + 1) * P], dft[:, t, :],
                                         start=(t == 0), stop=(t == TOK - 1))
                    last.then_inc(sems["freq"], 1)

                def side(k):
                    item = SIDE[k]
                    b = bank[6 + k % 2]
                    if k >= 2:
                        before = SIDE[k - 2][0]
                        if before == "s":
                            wait(pe, l, "square_mean", kind_before(k - 2, "s") + 1)
                        elif before == "w":
                            wait(pe, l, "added", adds_before(k - 2) + 1)
                        else:
                            wait(pe, l, "h_lo", 8 + kind_before(k - 2, "t") + 1)
                    if item[0] == "s":
                        g = item[1]
                        wait(pe, l, "square_added", g + 1)
                        if g == 0:
                            wait(pe, l, "conv_out", 2)
                        for t in range(TOK):
                            last = pe.matmul(b[:, t:t + 1], sqg[:, 0, t * P:(t + 1) * P], ones[:], start=True, stop=True)
                        last.then_inc(sems["square_sum"], 1)
                    elif item[0] == "w":
                        _, g, t, n = item
                        if (t, n) == (0, 0):
                            block_ready(l, IN_BLOCKS + g)
                        if g < 2:
                            wait(pe, l, "mix_lo", 2 * g + 2)
                        else:
                            wait(pe, l, "mix_lo", 4 + 4 * (g - 2) + t + 1)
                        for j in range(2):
                            c = 2 * g + j
                            last = three(b[:], mix_hi[:, c, t * P:(t + 1) * P], mix_lo[:, c, t * P:(t + 1) * P],
                                         *w_cols(IN_BLOCKS + g, j, D_MODEL, n * BANK, BANK), j == 0, j == 1)
                        last.then_inc(sems["products"], 1)
                    else:
                        _, t, half = item
                        turn_half(l, 1, t, half)

                side(0)
                for ct in range(2):
                    wait(pe, l, "freq_copied", ct + 1)
                    pe.matmul(bank[4 + ct][:, 0:HALF], head_dft[:, 0, :], freq[:, ct, 0:HALF], start=True, stop=True)
                    pe.matmul(bank[4 + ct][:, HALF:SEQ], head_dft[:, 1, :], freq[:, ct, HALF:SEQ],
                              start=True, stop=True).then_inc(sems["mixed"], 1)

                def turn_quad(q):
                    wait(pe, l, "out_gained", q + 1)
                    for j in range(2):
                        last = pe.transpose(bank[4 + q % 2][:, GROUP + j * P:GROUP + (j + 1) * P],
                                            head_gained[:, q % 2, j * P:(j + 1) * P], ident[:])
                    last.then_inc(sems["mix_turned"], 1)

                for s in range(STEPS):
                    if s < UNITS:
                        in_d, j, kv, qb, k0, k1 = unit(s)
                        if s == 0:
                            wait(pe, l, "k_lo", 2)
                        if s == 16:
                            wait(pe, l, "dq_lo", 2)
                        if s >= 2:
                            wait(pe, l, "probs", s - 1)
                        heads = slice(kv * HEAD_DIM, (kv + 1) * HEAD_DIM)
                        q, k = slice(qb * P, (qb + 1) * P), slice(k0 * P, k1 * P)
                        q_hi, q_lo = (dq_hi, dq_lo) if in_d else (aq_hi, aq_lo)
                        three(bank[s % 2][:, 0:(k1 - k0) * P], q_hi[heads, j, q], q_lo[heads, j, q],
                              (dk_hi if in_d else ak_hi)[heads, k], keys_lo[heads, 0 if in_d else 1, k], True, True)\
                            .then_inc(sems["scores"], 1)
                    if 0 <= s - TURN_LAG < UNITS:
                        u = s - TURN_LAG
                        _, _, _, _, k0, k1 = unit(u)
                        wait(pe, l, "probs", u + 1)
                        if u >= 2:
                            wait(pe, l, "prob_copied", u - 1)
                        for i in range(k1 - k0):
                            last = pe.transpose(bank[2 + u % 2][:, i * P:(i + 1) * P], stage[:, u % STAGES, i * P:(i + 1) * P], ident[:])
                        last.then_inc(sems["prob_turned"], 1)
                    for k in sides_of(s):
                        side(k)
                    if quad_turned_in(s) is not None:
                        turn_quad(quad_turned_in(s))
                    if s >= VALUE_LAG:
                        u = s - VALUE_LAG
                        in_d, j, kv, qb, k0, k1 = unit(u)
                        wait(pe, l, "prob_copied", u + 1)
                        if u == 0:
                            wait(pe, l, "fourier_out", 2)
                        if u % 4 == 0 and u >= 8:
                            wait(pe, l, "mix_lo", 4 + u // 4 - 1)
                        c = (2 * j + kv) * HEAD_DIM
                        for i in range(k1 - k0):
                            v = dv[:, k0 + i, kv * HEAD_DIM:(kv + 1) * HEAD_DIM] if in_d else \
                                tk[:, k0 + i, 2 * P + kv * HEAD_DIM:2 * P + (kv + 1) * HEAD_DIM]
                            last = pe.matmul(bank[4 + (u // 4) % 2][:, c:c + HEAD_DIM], pT[:, u % 2, i * P:(i + 1) * P], v,
                                             start=(i == 0), stop=(i == k1 - k0 - 1))
                        last.then_inc(sems["attended"], 1)

                def hidden(b, m, kt, t0, t1, first, last):
                    s_hi, s_lo = w_cols(b, kt, 2 * P, (m % 2) * P, P)
                    c = slice(t0 * P, t1 * P)
                    return three(bank[m][:, c], s_hi, s_lo, h_hi[:, kt, c], h_lo[:, kt, c], first, last)

                def rest_of_chunk(c, last_chunk):
                    def ready(i):
                        pe.wait_ge(sems["w_lo"], l * BLOCKS + c * CHUNK_BLOCKS + (MLP0 + i + 1))
                    for m in range(4, 8):
                        if m % 2 == 0:
                            ready(m // 2)
                        for kt in range(KT):
                            last = hidden(m // 2, m, kt, 0, TOK, kt == 0, kt == KT - 1)
                        last.then_inc(sems["products"], 1)
                    for g in range(8):
                        n, t = g // 4, g % 4
                        if last_chunk and g == 0:
                            pe.wait_ge(sems["relu"], l * 32 + c * KT + 5)
                        if last_chunk and g == 7:
                            turn(l + 1, 0)
                        for kt in range(KT):
                            i = 4 + 2 * n + kt // 4
                            if t == 0 and kt % 4 == 0:
                                ready(i)
                            if g == 0:
                                pe.wait_ge(sems["hidden_lo"], l * 32 + c * KT + (kt + 1))
                            last = three(chunk_bank(g, last_chunk)[:], hid_hi[:, kt, t * P:(t + 1) * P],
                                         hid_lo[:, kt, t * P:(t + 1) * P], *w_cols(i, kt % 4, BANK, 0, BANK), kt == 0, kt == KT - 1)
                        last.then_inc(sems["products"], 1)

                def hidden_early(m):
                    if m % 2 == 0:
                        block_ready(l, MLP0 + m // 2)
                    for kt in range(KT):
                        if m == 0 and kt == KT // 2:
                            turn_quad(7)
                        hidden(m // 2, m, kt, 0, 2, kt == 0, kt == KT - 1)

                wait(pe, l, "h_lo", 8 + 4)
                hidden_early(0)
                side(TAIL)
                side(TAIL + 1)
                hidden_early(1)
                side(TAIL + 2)
                side(TAIL + 3)
                hidden_early(2)
                side(TAIL + 4)
                side(TAIL + 5)
                hidden_early(3)
                wait(pe, l, "h_lo", 8 + 8)
                for m in range(4):
                    for kt in range(KT):
                        last = hidden(m // 2, m, kt, 2, 4, kt == 0, kt == KT - 1)
                    last.then_inc(sems["products"], 1)
                rest_of_chunk(0, False)

                def chunk(c, last_chunk):
                    pe.wait_ge(sems["added"], l * PER_LAYER["added"] + c * 8 + (32 - 4))
                    for kt in range(KT):
                        for m in range(4):
                            if kt == 0 and m % 2 == 0:
                                pe.wait_ge(sems["w_lo"], l * BLOCKS + c * CHUNK_BLOCKS + (MLP0 + m // 2 + 1))
                            last = hidden(m // 2, m, kt, 0, TOK, kt == 0, kt == KT - 1)
                            if kt == KT - 1:
                                last.then_inc(sems["products"], 1)
                    pe.wait_ge(sems["added"], l * PER_LAYER["added"] + c * 8 + 32)
                    rest_of_chunk(c, last_chunk)

                with pe.Fori(1, CHUNKS - 1) as c:
                    chunk(c, False)
                chunk(CHUNKS - 1, True)

        @block.scalar
        def _(act):
            act.dma_start(ident[:], ident_in).then_inc(ident_landed, 16)

            def split(l, b, released=None):
                act.wait_ge(w_landed[b % RAW], l * (16 * BLOCKS // RAW) + 16 * (b // RAW + 1))
                if released is not None:
                    wait(act, l, "products", released)
                act.copy(w_hi[:, b % RING, :], w_raw[:, b % RAW, :]).then_inc(sems["w_hi"], 1)

            def stream_high(l, which, t, half):
                wait(act, l, "turned", 8 * which + 2 * t + half + 1)
                src, dst = turned_half(which, t, half)
                act.copy(h_hi[dst], src).then_inc(sems["h_hi"], 1)

            def split_in_chunk(l, c, i, released):
                b = MLP0 + i
                act.wait_ge(w_landed[b % RAW], l * (16 * BLOCKS // RAW) + c * (16 * CHUNK_BLOCKS // RAW) + 16 * (b // RAW + 1))
                act.wait_ge(sems["products"], l * PER_LAYER["products"] + c * CHUNK_G + (MLP_G0 + released))
                act.copy(w_hi[:, b % RING, :], w_raw[:, b % RAW, :]).then_inc(sems["w_hi"], 1)

            act.wait_ge(const_set, 2)
            act.activation(neg_mx[:, 0:1], ones[:], ACT.Exp).then_inc(sems["table"], 1)
            split(0, 0)
            stream_high(0, 0, 0, 0)
            stream_high(0, 0, 0, 1)
            split(0, 1)
            with act.Fori(0, DEPTH) as l:
                for t in range(1, TOK):
                    stream_high(l, 0, t, 0)
                    stream_high(l, 0, t, 1)
                split(l, 2)
                split(l, 3)
                for t in range(TOK):
                    wait(act, l, "products", t + 1)
                    if t >= 2:
                        wait(act, l, "qk_sum", t - 1)
                    act.activation(sqd[:, t % 2, :], bank[t][:, 0:QK], ACT.Square).then_inc(sems["qk_square"], 1)
                    act.copy(dv[:, t, :], bank[t][:, QK:BANK]).then_inc(sems["dv_copied"], 1)
                split(l, 4, 4)
                split(l, 5, 4)
                for t in range(TOK):
                    wait(act, l, "products", 4 + t + 1)
                    act.copy(tk[:, t, :], bank[4 + t][:]).then_inc(sems["tk_copied"], 1)
                split(l, 6, 8)
                split(l, 7, 8)
                for j in range(2):
                    wait(act, l, "products", 8 + j + 1)
                    act.activation(aq_hi[:, j, :], bank[j][:], ACT.Copy, scale=HEAD_DIM ** -0.5).then_inc(sems["aq_hi"], 1)
                split(l, 8, 10)
                for j in range(2):
                    wait(act, l, "products", 10 + j + 1)
                    act.copy(bz[:, j, :], bank[2 + j][:]).then_inc(sems["bu_copied"], 1)
                split(l, 9, 12)
                split(l, 10, 14)
                split(l, 11, 16)

                def square(j, src):
                    act.activation(sqg[:, j, :], src, ACT.Square).then_inc(sems["group_square"], 1)

                def mix_high(g, j, src):
                    c = 2 * g + j
                    act.activation(mix_hi[:, c, :], src, ACT.Copy, scale=cols[:, COL_GRP + c:COL_GRP + c + 1]).then_inc(sems["mix_hi"], 1)

                for j in range(2):
                    wait(act, l, "qk_turned", 3 + j)
                    act.copy((dk_hi, ak_hi)[j][:], bank[2 + j][:]).then_inc(sems["k_hi"], 1)
                for j in range(2):
                    act.copy(dq[:, j, :], bank[j][:]).then_inc(sems["dq_copied"], 1)
                for j in range(2):
                    wait(act, l, "conv_out", j + 1)
                    square(j, bo[:, j, :])
                    mix_high(0, j, bo[:, j, :])
                for ct in range(2):
                    wait(act, l, "freq", ct + 1)
                    wait(act, l, "qk_roped", TOK)
                    act.copy(freq[:, ct, :], bank[4 + ct][:]).then_inc(sems["freq_copied"], 1)
                for ct in range(2):
                    wait(act, l, "mixed", ct + 1)
                    act.copy(sine[:, ct, :], bank[4 + ct][:, HALF:SEQ]).then_inc(sems["sine_copied"], 1)

                def square_head_out(q):
                    wait(act, l, "head_out", q + 1)
                    if q >= 1:
                        wait(act, l, "out_square", q)
                    act.activation(head_square[:], head_out[:, q % 2, :], ACT.Square,
                                   accum_out=head_ss[:, q % 2:q % 2 + 1]).then_inc(sems["out_square"], 1)

                def mix_high_quad(q):
                    wait(act, l, "mix_turned", q + 1)
                    src, dst = turned_quad(q)
                    act.copy(mix_hi[dst], src).then_inc(sems["mix_hi"], 1)

                def side(k):
                    if SIDE[k][0] == "t":
                        stream_high(l, 1, SIDE[k][1], SIDE[k][2])

                def split_half(b, half, released):
                    if half == 0:
                        act.wait_ge(w_landed[b % RAW], l * (16 * BLOCKS // RAW) + 16 * (b // RAW + 1))
                        wait(act, l, "products", released)
                    c = slice(half * BLOCK // 2, (half + 1) * BLOCK // 2)
                    done = act.copy(w_hi[:, b % RING, c], w_raw[:, b % RAW, c])
                    if half == 1:
                        done.then_inc(sems["w_hi"], 1)

                for s in range(STEPS):
                    if quad_turned_in(s) is not None:
                        square_head_out(quad_turned_in(s))
                    if 0 <= s - TURN_LAG < UNITS:
                        u = s - TURN_LAG
                        _, _, _, _, k0, k1 = unit(u)
                        wait(act, l, "prob_turned", u + 1)
                        if u >= 2:
                            wait(act, l, "attended", u - 1)
                        act.copy(pT[:, u % 2, 0:(k1 - k0) * P], bank[2 + u % 2][:, 0:(k1 - k0) * P]).then_inc(sems["prob_copied"], 1)
                    if s < UNITS:
                        in_d, j, kv, qb, k0, k1 = unit(s)
                        n = (k1 - k0) * P
                        quad, i = (s // 4) % 2, s % 4
                        bias = neg_mx[:, s % 2:s % 2 + 1]
                        wait(act, l, "neg_max", s + 1)
                        if in_d:
                            wait(act, l, "prob_turned", s - STAGES + 1)
                            act.activation(stage[:, s % STAGES, 0:n], bank[s % 2][:, 0:n], ACT.Exp, bias=bias,
                                           scale=HEAD_DIM ** -0.5, accum_out=p_sum[:, quad, i:i + 1]).then_inc(sems["probs"], 1)
                        else:
                            head = head_of(j, kv)
                            act.activation(sink_e[:, quad, i:i + 1], cols[:, COL_SINK + head:COL_SINK + head + 1], ACT.Exp,
                                           bias=bias).then_inc(sems["sink_exp"], 1)
                            act.activation(stage[:, s % STAGES, 0:n], stage[:, s % STAGES, 0:n], ACT.Exp, bias=bias,
                                           accum_out=p_sum[:, quad, i:i + 1]).then_inc(sems["probs"], 1)
                    if s in (1, 2):
                        j = s - 1
                        wait(act, l, "fourier_out", j + 1)
                        wait(act, l, "square_sum", 1)
                        square(j, co[:, j, :])
                        mix_high(1, j, co[:, j, :])
                    if s in (5, 6):
                        j = s - 5
                        wait(act, l, "mix_lo", 2)
                        wait(act, l, "dq_copied", j + 1)
                        act.copy(dq_hi[:, j, :], dq[:, j, :]).then_inc(sems["dq_hi"], 1)
                    for k in sides_of(s):
                        side(k)
                    if quad_turned_in(s) is not None:
                        mix_high_quad(quad_turned_in(s))
                    if s in (10, 11):
                        split_half(12, s - 10, 24)
                    if s in (18, 19):
                        split_half(13, s - 18, 32)
                square_head_out(7)
                mix_high_quad(7)
                for k in range(TAIL, len(SIDE)):
                    side(k)

                def chunk(c, before_second_half):
                    split_in_chunk(l, c, 2, 0)
                    split_in_chunk(l, c, 3, 0)
                    for m in range(8):
                        act.wait_ge(sems["products"], l * PER_LAYER["products"] + c * CHUNK_G + (MLP_G0 + m + 1))
                        if m >= 2:
                            act.wait_ge(sems["hidden_square"], l * 32 + c * KT + (m - 1))
                            act.wait_ge(sems["hidden_hi"], l * 32 + c * KT + (m - 1))
                        act.activation(stage[:, m % 2, :], bank[m][:], ACT.Relu, scale=ALPHA ** -0.5).then_inc(sems["relu"], 1)
                        act.wait_ge(sems["relu"], l * 32 + c * KT + (m + 1))
                        act.activation(hid_hi[:, m, :], stage[:, m % 2, :], ACT.Square).then_inc(sems["hidden_hi"], 1)
                        if m == 3:
                            split_in_chunk(l, c, 4, 4)
                            split_in_chunk(l, c, 5, 4)
                        if m == 5:
                            split_in_chunk(l, c, 6, 6)
                        if m == 7:
                            split_in_chunk(l, c, 7, 8)
                    before_second_half()

                with act.Fori(0, CHUNKS - 1) as c:
                    def next_chunk():
                        split_in_chunk(l, c, 8, 12)
                        split_in_chunk(l, c, 9, 12)
                    chunk(c, next_chunk)
                chunk(CHUNKS - 1, lambda: None)
                with act.If(l < DEPTH - 1):
                    split(l + 1, 0, 12 - CHUNK_G)
                    split(l + 1, 1, 12 - CHUNK_G)
                stream_high(l + 1, 0, 0, 0)
                stream_high(l + 1, 0, 0, 1)

        @block.vector
        def _(dve):
            dve.memset(ones[:], 1.0).then_inc(const_set, 1)
            dve.memset(half_neg[:], -0.5).then_inc(const_set, 1)
            def split(l, b):
                wait(dve, l, "w_hi", b + 1)
                dve.tensor_tensor(w_lo[:, b % RING, :], w_raw[:, b % RAW, :], w_hi[:, b % RING, :].bitcast(F32),
                                  ALU.subtract).then_inc(sems["w_lo"], 1)

            def split_in_chunk(l, c, i):
                b = MLP0 + i
                dve.wait_ge(sems["w_hi"], l * BLOCKS + c * CHUNK_BLOCKS + (b + 1))
                dve.tensor_tensor(w_lo[:, b % RING, :], w_raw[:, b % RAW, :], w_hi[:, b % RING, :].bitcast(F32),
                                  ALU.subtract).then_inc(sems["w_lo"], 1)

            def row_stats(t, n):
                dve.bn_stats(bn[:, t, n, :], x[:, t, n * BANK:(n + 1) * BANK]).then_inc(sems["stats"], 1)

            def variance(k, t, stats_done):
                counted = dve.to_reg(8 * k + stats_done)
                dve.wait_ge(x_landed[t], 16)
                dve.wait_ge(sems["stats"], counted)
                dve.bn_aggr(moments[:, t, :], bn[:, t, :, :].rearrange("p a b -> p (a b)")).then_inc(sems["moments"], 1)
                dve.wait_ge(sems["moments"], 4 * k + (t + 1))
                eps = LN_EPS / ALPHA ** 2 if not isinstance(k, int) or k else LN_EPS
                dve.tensor_scalar(var_eps[:, t:t + 1], moments[:, t, 1:2], eps, None, ALU.add).then_inc(sems["var_ready"], 1)

            def centre(k, t):
                dve.wait_ge(sems["moments"], 4 * k + (t + 1))
                dve.wait_ge(sems["rows"], 16 * k + 16)
                dve.scalar_tensor_tensor(out=x[:, t, :], in0=x[:, t, :], scalar=moments[:, t, 0:1], in1=rows[:, 0:D_MODEL],
                                         op0=ALU.subtract, op1=ALU.mult).then_inc(sems["centred"], 1)

            def scale(k, t):
                dve.wait_ge(sems["rstd"], 4 * k + (t + 1))
                dve.wait_ge(sems["centred"], 4 * k + (t + 1))
                for half in range(2):
                    c = slice(half * BANK, (half + 1) * BANK)
                    dve.scalar_tensor_tensor(out=x[:, t, c], in0=x[:, t, c], scalar=rstd[:, t:t + 1],
                                             in1=rows[:, D_MODEL + half * BANK:D_MODEL + (half + 1) * BANK],
                                             op0=ALU.mult, op1=ALU.add).then_inc(sems["normed"], 1)

            def normalise(k, t):
                centre(k, t)
                scale(k, t)

            def low_half(l, which, t, half):
                wait(dve, l, "h_hi", 8 * which + 2 * t + half + 1)
                src, dst = turned_half(which, t, half)
                dve.tensor_tensor(h_lo[dst], src, h_hi[dst].bitcast(F32), ALU.subtract).then_inc(sems["h_lo"], 1)

            def stream_low(l, which, t):
                low_half(l, which, t, 0)
                low_half(l, which, t, 1)

            def input_stats(t):
                dve.wait_ge(x_landed[t], 16)
                row_stats(t, 0)
                row_stats(t, 1)
                variance(0, t, 2 * t + 2)

            input_stats(0)
            normalise(0, 0)
            input_stats(1)
            stream_low(0, 0, 0)
            normalise(0, 1)
            dve.wait_ge(sems["w_lo"], 1)
            split(0, 1)
            stream_low(0, 0, 1)
            input_stats(2)
            normalise(0, 2)
            input_stats(3)
            stream_low(0, 0, 2)
            normalise(0, 3)

            with dve.Fori(0, DEPTH) as l:
                dve.wait_ge(sems["param"], l * 32 + 32)
                stream_low(l, 0, 3)
                split(l, 2)
                split(l, 3)
                for t in range(TOK):
                    wait(dve, l, "products", t + 1)
                    wait(dve, l, "qk_square", t + 1)
                    wait(dve, l, "dv_copied", t + 1)
                    dve.tensor_tensor(qkr[:, t, :], bank[t][:, 0:QK], qk_gain[:], ALU.mult).then_inc(sems["qk_gain"], 1)
                    dve.tensor_reduce(qk_ss[:, t, :], sqd[:, t % 2, :].rearrange("p (h d) -> p h d", h=QK_HEADS), AX_X, ALU.add)\
                       .then_inc(sems["qk_sum"], 1)
                    wait(dve, l, "qk_sum", t + 1)
                    dve.tensor_scalar(qk_ss[:, t, :], qk_ss[:, t, :], 1.0 / HEAD_DIM, RMS_EPS, ALU.mult, ALU.add)\
                       .then_inc(sems["qk_eps"], 1)
                split(l, 4)
                split(l, 5)
                wait(dve, l, "qk_rstd", 1)
                dve.wait_ge(const_landed, 16 * 4)
                for t in range(TOK):
                    heads = qkr[:, t, :].rearrange("p (h d) -> p h d", h=QK_HEADS)
                    dve.tensor_tensor(heads, heads, qk_r[:, t, :].unsqueeze(2).to_broadcast([P, QK_HEADS, HEAD_DIM]),
                                      ALU.mult).then_inc(sems["qk_unit"], 1)
                for t in range(TOK):
                    heads = qkr[:, t, :].rearrange("p (h d) -> p h d", h=QK_HEADS)
                    wait(dve, l, "qk_unit", t + 1)
                    if t >= 1:
                        wait(dve, l, "qk_roped", t)
                    dve.tensor_tensor(rope_a[:].rearrange("p (h d) -> p h d", h=QK_HEADS), heads,
                                      rope[:, 0:1, t, :].to_broadcast([P, QK_HEADS, HEAD_DIM]), ALU.mult).then_inc(sems["rope_cos"], 1)
                    m = AXIS_DIM // 2
                    quarters = qkr[:, t, :].rearrange("p (h f m) -> p h f m", h=2 * QK_HEADS, f=2)
                    turned = rope_b[:].rearrange("p (h f m) -> p h f m", h=2 * QK_HEADS, f=2)
                    for f in range(2):
                        sines = rope[:, 1, t, :].rearrange("p (a f m) -> p a f m", a=2, f=2)[:, :, f, :]
                        for_heads = sines.unsqueeze(1).to_broadcast([P, QK_HEADS, 2, m])
                        src = quarters[:, :, 1 - f, :].rearrange("p (h a) m -> p h a m", a=2)
                        dst = turned[:, :, f, :].rearrange("p (h a) m -> p h a m", a=2)
                        dve.tensor_tensor(dst, src, for_heads, ALU.mult).then_inc(sems["rope_sin"], 1)
                    wait(dve, l, "rope_cos", t + 1)
                    wait(dve, l, "rope_sin", 2 * t + 2)
                    dve.tensor_tensor(qkr[:, t, :], rope_a[:], rope_b[:], ALU.add).then_inc(sems["qk_roped"], 1)
                split(l, 6)
                split(l, 7)
                for j in range(2):
                    wait(dve, l, "aq_hi", j + 1)
                    dve.scalar_tensor_tensor(out=aq_lo[:, j, :], in0=bank[j][:], scalar=HEAD_DIM ** -0.5, in1=aq_hi[:, j, :].bitcast(F32),
                                             op0=ALU.mult, op1=ALU.subtract).then_inc(sems["aq_lo"], 1)
                split(l, 8)
                split(l, 9)
                for j in range(2):
                    wait(dve, l, "products", 12 + j + 1)
                    wait(dve, l, "bu_copied", j + 1)
                    z, o = bz[:, j, :], bo[:, j, :]
                    tap = [cols[:, COL_CONV + 2 * i + j:COL_CONV + 2 * i + j + 1] for i in range(3)]
                    dve.tensor_tensor(z, bank[4 + j][:], z, ALU.mult).then_inc(sems["conv_step"], 1)
                    wait(dve, l, "conv_step", 4 * j + 1)
                    dve.tensor_scalar(o, z, tap[1], None, ALU.mult).then_inc(sems["conv_step"], 1)
                    wait(dve, l, "conv_step", 4 * j + 2)
                    dve.scalar_tensor_tensor(out=o[:, 1:SEQ], in0=z[:, 0:SEQ - 1], scalar=tap[0], in1=o[:, 1:SEQ],
                                             op0=ALU.mult, op1=ALU.add).then_inc(sems["conv_step"], 1)
                    wait(dve, l, "conv_step", 4 * j + 3)
                    dve.scalar_tensor_tensor(out=o[:, 0:SEQ - 1], in0=z[:, 1:SEQ], scalar=tap[2], in1=o[:, 0:SEQ - 1],
                                             op0=ALU.mult, op1=ALU.add).then_inc(sems["conv_step"], 1)
                split(l, 10)
                for j in range(2):
                    wait(dve, l, "products", 14 + j + 1)
                    wait(dve, l, "conv_step", 4 * j + 4)
                    dve.tensor_tensor(bo[:, j, :], bank[6 + j][:], bo[:, j, :], ALU.mult).then_inc(sems["conv_out"], 1)
                for j in range(2):
                    wait(dve, l, "k_hi", j + 1)
                    dve.tensor_tensor(keys_lo[:, j, :], bank[2 + j][:], (dk_hi, ak_hi)[j][:].bitcast(F32), ALU.subtract)\
                       .then_inc(sems["k_lo"], 1)
                split(l, 11)

                def mix_low(g, j, src):
                    c = 2 * g + j
                    wait(dve, l, "mix_hi", c + 1)
                    dve.scalar_tensor_tensor(out=mix_lo[:, c, :], in0=src, scalar=cols[:, COL_GRP + c:COL_GRP + c + 1],
                                             in1=mix_hi[:, c, :].bitcast(F32), op0=ALU.mult, op1=ALU.subtract).then_inc(sems["mix_lo"], 1)

                def mean_square(dst, src, done):
                    dve.tensor_scalar(dst, src, ALPHA ** 2 / GROUP, ALPHA ** 2 * RMS_EPS, ALU.mult, ALU.add).then_inc(sems["square_mean"], 1)

                def scale_quad(q):
                    b = q % 2
                    wait(dve, l, "attended", 4 * q + 4)
                    total = p_sum[:, b, :]
                    if q < 4:
                        dve.tensor_tensor(den[:, b, :], p_sum[:, b, :], sink_e[:, b, :], ALU.add).then_inc(sems["denom"], 1)
                        wait(dve, l, "denom", q + 1)
                        total = den[:, b, :]
                    dve.reciprocal(inv[:, b, :], total).then_inc(sems["inv_denom"], 1)
                    wait(dve, l, "inv_denom", q + 1)
                    if q >= 2:
                        wait(dve, l, "out_square", q - 1)
                        wait(dve, l, "out_gained", q - 1)
                    dve.tensor_tensor(head_out[:, b, :].rearrange("p (h d) -> p h d", h=4),
                                      bank[4 + b][:, 0:GROUP].rearrange("p (h d) -> p h d", h=4),
                                      inv[:, b, :].unsqueeze(2).to_broadcast([P, 4, HEAD_DIM]), ALU.mult).then_inc(sems["head_out"], 1)

                def mix_low_quad(q):
                    g, t = 2 + q // 4, q % 4
                    wait(dve, l, "out_square", q + 1)
                    mean_square(mean_sq[:, g, t:t + 1], head_ss[:, q % 2:q % 2 + 1], q)
                    wait(dve, l, "mix_hi", 4 + q + 1)
                    src, dst = turned_quad(q)
                    dve.tensor_tensor(mix_lo[dst], src, mix_hi[dst].bitcast(F32), ALU.subtract).then_inc(sems["mix_lo"], 1)

                mix_low(0, 0, bo[:, 0, :])
                mix_low(0, 1, bo[:, 1, :])
                def side(k):
                    item = SIDE[k]
                    b = bank[6 + k % 2]
                    if item[0] == "s":
                        g = item[1]
                        wait(dve, l, "square_sum", g + 1)
                        mean_square(mean_sq[:, g, :], b[:, 0:TOK], g)
                    elif item[0] == "w":
                        _, g, t, n = item
                        wait(dve, l, "products", 16 + adds_before(k) + 1)
                        if n == 0:
                            wait(dve, l, "group_rstd", g + 1 if g < 2 else 2 + 4 * (g - 2) + t + 1)
                        if last_add(k):
                            wait(dve, l, "added", last_add(k))
                        xs = x[:, t, n * BANK:(n + 1) * BANK]
                        dve.scalar_tensor_tensor(out=xs, in0=b[:], scalar=group_r[:, g, t:t + 1], in1=xs, op0=ALU.mult, op1=ALU.add)\
                           .then_inc(sems["added"], 1)
                        if g == 3:
                            wait(dve, l, "added", adds_before(k) + 1)
                            row_stats(t, n)
                            if n == 1:
                                variance(2 * l + 1, t, 2 * t + 2)
                    else:
                        low_half(l, 1, item[1], item[2])

                side(0)
                for ct in range(2):
                    wait(dve, l, "sine_copied", ct + 1)
                    cosine, o = bank[4 + ct], co[:, ct, :]
                    dve.tensor_tensor(o[:, 1:HALF - 1], cosine[:, 1:HALF - 1], sine[:, ct, :], ALU.subtract).then_inc(sems["fourier_step"], 1)
                    dve.tensor_tensor(o[:, SEQ - 1:HALF - 1:-1], cosine[:, 1:HALF - 1], sine[:, ct, :], ALU.add).then_inc(sems["fourier_step"], 1)
                    dve.tensor_copy(o[:, 0:HALF:HALF - 1], cosine[:, 0:HALF:HALF - 1]).then_inc(sems["fourier_out"], 1)

                for s in range(STEPS):
                    if s < UNITS:
                        in_d, j, kv, qb, k0, k1 = unit(s)
                        n = (k1 - k0) * P
                        sl = slice(s % 2, s % 2 + 1)
                        wait(dve, l, "scores", s + 1)
                        if s >= 2:
                            wait(dve, l, "probs", s - 1)
                        if not in_d:
                            head = head_of(j, kv)
                            if s >= STAGES:
                                wait(dve, l, "prob_turned", s - STAGES + 1)
                            d0 = (k0 - qb + 1) * P
                            dve.scalar_tensor_tensor(out=stage[:, s % STAGES, 0:n], in0=dist[:, d0:d0 + n], scalar=2.0 ** (-8.0 * (head + 1) / A_HEADS),
                                                     in1=bank[s % 2][:, 0:n], op0=ALU.mult, op1=ALU.add).then_inc(sems["biased"], 1)
                            wait(dve, l, "biased", s + 1)
                            dve.reduce_max(mx[:, sl], stage[:, s % STAGES, 0:n], AX_X).then_inc(sems["row_max"], 1)
                            wait(dve, l, "row_max", s + 1)
                            dve.tensor_scalar(neg_mx[:, sl], mx[:, sl], cols[:, COL_SINK + head:COL_SINK + head + 1], -1.0,
                                              ALU.max, ALU.mult).then_inc(sems["neg_max"], 1)
                        else:
                            dve.reduce_max(mx[:, sl], bank[s % 2][:, 0:n], AX_X).then_inc(sems["row_max"], 1)
                            wait(dve, l, "row_max", s + 1)
                            dve.tensor_scalar(neg_mx[:, sl], mx[:, sl], -HEAD_DIM ** -0.5, None, ALU.mult).then_inc(sems["neg_max"], 1)
                    for k in sides_of(s):
                        side(k)
                    if s in (2, 3):
                        mix_low(1, s - 2, co[:, s - 2, :])
                    if quad_turned_in(s) is not None:
                        mix_low_quad(quad_turned_in(s))
                    if quad_scaled_in(s) is not None:
                        scale_quad(quad_scaled_in(s))
                    if s in NORM_AT:
                        centre(2 * l + 1, NORM_AT[s])
                    if s - 1 in NORM_AT:
                        scale(2 * l + 1, NORM_AT[s - 1])
                centre(2 * l + 1, 2)
                mix_low_quad(7)
                scale(2 * l + 1, 2)
                side(TAIL)
                side(TAIL + 1)
                centre(2 * l + 1, 3)
                side(TAIL + 2)
                side(TAIL + 3)
                scale(2 * l + 1, 3)
                wait(dve, l, "w_lo", 14)
                side(TAIL + 4)
                side(TAIL + 5)

                def chunk(c, last):
                    split_in_chunk(l, c, 2)
                    split_in_chunk(l, c, 3)
                    for m in range(9):
                        if m < 8:
                            dve.wait_ge(sems["relu"], l * 32 + c * KT + (m + 1))
                            if m >= 2:
                                dve.wait_ge(sems["hidden_lo"], l * 32 + c * KT + (m - 1))
                            r = stage[:, m % 2, :]
                            dve.tensor_tensor(y[:, m % 2, :], r, r, ALU.mult).then_inc(sems["hidden_square"], 1)
                        if m >= 1:
                            i = m - 1
                            dve.wait_ge(sems["hidden_hi"], l * 32 + c * KT + (i + 1))
                            dve.wait_ge(sems["hidden_square"], l * 32 + c * KT + (i + 1))
                            dve.tensor_tensor(hid_lo[:, i, :], y[:, i % 2, :], hid_hi[:, i, :].bitcast(F32), ALU.subtract)\
                               .then_inc(sems["hidden_lo"], 1)
                        if m == 4:
                            split_in_chunk(l, c, 4)
                            split_in_chunk(l, c, 5)
                        if m == 6:
                            split_in_chunk(l, c, 6)
                        if m == 8:
                            split_in_chunk(l, c, 7)
                    for g in range(8):
                        n, t = g // 4, g % 4
                        dve.wait_ge(sems["products"], l * PER_LAYER["products"] + c * CHUNK_G + (MLP_G0 + 8 + g + 1))
                        if g == 0:
                            dve.wait_ge(sems["added"], l * PER_LAYER["added"] + c * 8 + 32)
                        xs = x[:, t, n * BANK:(n + 1) * BANK]
                        dve.tensor_tensor(xs, chunk_bank(g, last)[:], xs, ALU.add).then_inc(sems["added"], 1)
                        if g == 3 and not last:
                            split_in_chunk(l, c, 8)
                            split_in_chunk(l, c, 9)
                        if last and g == 3:
                            with dve.If(l < DEPTH - 1):
                                split(l + 1, 0)
                                split(l + 1, 1)
                        if last:
                            wait(dve, l, "added", 32 + 8 * (CHUNKS - 1) + g + 1)
                            row_stats(t, n)
                            if n == 1:
                                variance(2 * l + 2, t, 4 + t + 1)
                                normalise(2 * l + 2, t)
                            if g == 6:
                                stream_low(l + 1, 0, 0)

                with dve.Fori(0, CHUNKS - 1) as c:
                    chunk(c, False)
                chunk(CHUNKS - 1, True)
                with dve.If(l < DEPTH - 1):
                    stream_low(l + 1, 0, 1)
                    stream_low(l + 1, 0, 2)

        @block.gpsimd
        def _(pool):
            def load_params(l):
                pool.dma_start(cols[:], cols_in[bass.ds(l, 1)].rearrange("a p n -> p (a n)")).then_inc(sems["param"], 16)
                pool.dma_start(qk_gain[:], qk_gain_in[bass.ds(l, 1)].to_broadcast([P, QK])).then_inc(sems["param"], 16)

            def load_rows(k):
                if not isinstance(k, int):
                    pool.wait_ge(sems["normed"], 8 * k)
                pool.dma_start(rows[:], rows_in[bass.ds(k, 1)].to_broadcast([P, 2 * D_MODEL])).then_inc(sems["rows"], 16)

            def power(dst, src, n):
                return pool.tensor_tensor(dst, src, half_neg[:, 0:n], ALU.pow)

            def layer_norm_rstd(k, t0=0, t1=TOK):
                for t in range(t0, t1):
                    pool.wait_ge(sems["var_ready"], 4 * k + (t + 1))
                    power(rstd[:, t:t + 1], var_eps[:, t:t + 1], 1).then_inc(sems["rstd"], 1)

            def split_low(l, b):
                wait(pool, l, "w_hi", b + 1)
                pool.tensor_tensor(w_lo[:, b % RING, :], w_raw[:, b % RAW, :], w_hi[:, b % RING, :].bitcast(F32),
                                   ALU.subtract).then_inc(sems["w_lo"], 1)

            load_rows(0)
            load_params(0)
            pool.wait_ge(const_set, 2)
            layer_norm_rstd(0, 0, 1)
            split_low(0, 0)
            layer_norm_rstd(0, 1)
            with pool.Fori(0, DEPTH) as l:
                wait(pool, l, "qk_eps", TOK)
                power(qk_r[:].rearrange("p t h -> p (t h)"), qk_ss[:].rearrange("p t h -> p (t h)"), TOK * QK_HEADS)\
                    .then_inc(sems["qk_rstd"], 1)
                wait(pool, l, "conv_step", 8)
                pool.dma_start(head_gain[:].rearrange("p g n -> p (g n)"), head_gain_in[bass.ds(l, 1)].to_broadcast([P, 2 * GROUP]))\
                    .then_inc(sems["head_gain"], 16)
                for g in range(2):
                    wait(pool, l, "group_square", 2 * g + 2)
                    pool.tensor_tensor(sqg[:, 0, :], sqg[:, 0, :], sqg[:, 1, :], ALU.add).then_inc(sems["square_added"], 1)
                    wait(pool, l, "square_mean", g + 1)
                    power(group_r[:, g, :], mean_sq[:, g, :], TOK).then_inc(sems["group_rstd"], 1)

                wait(pool, l, "head_gain", 16)
                for q in range(8):
                    g, t = q // 4, q % 4
                    if q >= 5:
                        layer_norm_rstd(2 * l + 1, q - 5, q - 4)
                    wait(pool, l, "head_out", q + 1)
                    if q >= 2:
                        wait(pool, l, "mix_turned", q - 1)
                    pool.tensor_tensor(head_gained[:, q % 2, :], head_out[:, q % 2, :], head_gain[:, g, :], ALU.mult)\
                        .then_inc(sems["out_gained"], 1)
                    wait(pool, l, "square_mean", 2 + q + 1)
                    power(group_r[:, 2 + g, t:t + 1], mean_sq[:, 2 + g, t:t + 1], 1).then_inc(sems["group_rstd"], 1)
                    if q == 0:
                        for j in range(2):
                            wait(pool, l, "dq_hi", j + 1)
                            pool.tensor_tensor(dq_lo[:, j, :], dq[:, j, :], dq_hi[:, j, :].bitcast(F32), ALU.subtract).then_inc(sems["dq_lo"], 1)
                    if q == 2:
                        split_low(l, 12)
                    if q == 3:
                        load_rows(2 * l + 1)
                    if q == 4:
                        split_low(l, 13)
                layer_norm_rstd(2 * l + 1, TOK - 1)
                load_params(l + 1)
                load_rows(2 * l + 2)
                layer_norm_rstd(2 * l + 2)


def lay_out(x, ln_in_g, ln_in_b, w_in, conv_w, sink, qn_g, kn_g, grp_g, w_out, ln1_g, ln1_b, w1, w2, ln2_g, ln2_b):
    a = {k: np.asarray(v) for k, v in dict(
        x=x, ln_in_g=ln_in_g, ln_in_b=ln_in_b, w_in=w_in, conv_w=conv_w, sink=sink, qn_g=qn_g, kn_g=kn_g, grp_g=grp_g,
        w_out=w_out, ln1_g=ln1_g, ln1_b=ln1_b, w1=w1, w2=w2, ln2_g=ln2_g, ln2_b=ln2_b).items()}
    lane = np.arange(HEAD_DIM)
    heads = np.concatenate([head_of(j, kv) * HEAD_DIM + lane for j in range(2) for kv in range(2)])
    order = dict(a_q=0, a_k=256, a_v=384, b_u=512, b_gate=768, c_gate=1024, c_u=1280, d_q=1536, d_k=1792, d_v=1920)

    def columns(name, n, perm=None):
        return order[name] + (np.arange(n) if perm is None else perm)

    def tiles(w, n_rows, width):
        return w.reshape(n_rows, P, width).transpose(1, 0, 2).reshape(P, n_rows * width)

    weights = np.empty((DEPTH * BLOCKS, P, BLOCK), np.float32)
    cols = np.empty((DEPTH + 1, P, N_COLS), np.float32)
    for l in range(DEPTH + 1):
        m = min(l, DEPTH - 1)
        grp = a["grp_g"][m].reshape(4, GROUP)
        for c, v in ((COL_CONV, a["conv_w"][m].reshape(-1)), (COL_GRP, np.concatenate([grp[1], grp[2]]))):
            cols[l, :, c:c + v.size // P] = v.reshape(-1, P).T
        cols[l, :, COL_SINK:] = a["sink"][m][None, :]
    for l in range(DEPTH):
        blocks = weights[l * BLOCKS:(l + 1) * BLOCKS]
        w = a["w_in"][l]
        token_major = [np.concatenate([columns("d_q", 256, heads), columns("d_k", P), columns("d_v", P)]),
                       np.concatenate([columns("c_u", 256), columns("a_v", P), columns("a_k", P)])]
        for i, c in enumerate(token_major):
            for j in range(2):
                blocks[2 * i + j] = tiles(w[j * 512:(j + 1) * 512, c], 4, BANK)
        channel_major = [columns("a_q", 256, heads), columns("b_u", 256), columns("c_gate", 256), columns("b_gate", 256)]
        for i, c in enumerate(channel_major):
            blocks[4 + i] = tiles(w[:, c], KT, 2 * P)
        wo = a["w_out"][l].reshape(4, GROUP, D_MODEL)
        for i, g in enumerate([wo[1], wo[2], wo[0][heads], wo[3][heads]]):
            blocks[IN_BLOCKS + i] = tiles(g, 2, D_MODEL)
        for c in range(CHUNKS):
            first = MLP0 + c * CHUNK_BLOCKS
            for i in range(4):
                lo = c * 1024 + i * 256
                blocks[first + i] = tiles(a["w1"][l][:, lo:lo + 256], KT, 256)
            for i in range(4):
                n, k = i // 2, i % 2
                lo = c * 1024 + k * 512
                blocks[first + 4 + i] = tiles(a["w2"][l][lo:lo + 512, n * BANK:(n + 1) * BANK], 4, BANK)
    rows = np.stack([np.concatenate([a["ln_in_g"], a["ln_in_b"]])]
                    + [np.concatenate([a[f"{n}_g"][l], a[f"{n}_b"][l]]) for l in range(DEPTH) for n in ("ln1", "ln2")])
    qk_gain = np.stack([np.concatenate([np.tile(a["qn_g"][l], 4), np.tile(a["kn_g"][l], 2)])
                        for l in list(range(DEPTH)) + [DEPTH - 1]])
    grp = a["grp_g"].reshape(DEPTH, 4, GROUP)
    head_gain = np.stack([np.concatenate([grp[l, 0][heads], grp[l, 3][heads]]) for l in range(DEPTH)])
    f32 = np.float32
    inv_freq = (f32(ROPE_THETA) ** (-np.arange(0, AXIS_DIM, 2, dtype=f32) / f32(AXIS_DIM))).astype(f32)
    tok = np.arange(SEQ)
    angle = np.stack([(tok // GRID_W).astype(f32)[:, None] * inv_freq, (tok % GRID_W).astype(f32)[:, None] * inv_freq], 1)
    angle = angle.astype(np.float64)
    cosine = np.stack([np.cos(angle), np.cos(angle)], 2).reshape(SEQ, HEAD_DIM)
    sine = np.stack([-np.sin(angle), np.sin(angle)], 2).reshape(SEQ, HEAD_DIM)
    rope = np.stack([cosine, sine]).reshape(2, TOK, P, HEAD_DIM).transpose(2, 0, 1, 3).astype(f32)
    gap = np.abs(np.arange(P)[:, None] + P - np.arange(3 * P)[None, :])
    dist = np.where(gap <= WINDOW, -gap, -1e33).astype(f32)
    turn = 2 * np.pi * (np.outer(tok, tok) % SEQ) / SEQ
    dft = np.concatenate([np.cos(turn[:, :HALF]), np.sin(turn[:, 1:HALF - 1])], 1) / np.sqrt(SEQ)
    dft = dft.reshape(TOK, P, SEQ).transpose(1, 0, 2).astype(f32)
    turn = 2 * np.pi * (np.outer(lane, lane) % HEAD_DIM) / HEAD_DIM
    head_dft = np.zeros((P, 2, P))
    for h in range(2):
        sl = slice(h * HEAD_DIM, (h + 1) * HEAD_DIM)
        head_dft[sl, 0, sl] = np.cos(turn) / np.sqrt(HEAD_DIM)
        head_dft[sl, 1, sl] = np.sin(turn) / np.sqrt(HEAD_DIM)
    return dict(x=a["x"].reshape(TOK, P, D_MODEL), weights=weights, cols=cols, rows=rows,
                qk_gain=qk_gain, head_gain=head_gain, rope=np.ascontiguousarray(rope), dist=dist, dft=np.ascontiguousarray(dft),
                head_dft=head_dft.astype(f32), ident=np.eye(P, dtype=f32))


def kernel(**inputs):
    import concourse.bacc as bacc
    from concourse.bass_utils import run_bass_kernel_spmd

    nc = bacc.Bacc("TRN2", target_bir_lowering=False, num_devices=1)
    arrays, args = {}, []
    for name, array in lay_out(**inputs).items():
        arrays[f"in_{name}"] = np.ascontiguousarray(array)
        args.append(nc.dram_tensor(f"in_{name}", array.shape, mybir.dt.from_np(array.dtype), kind="ExternalInput").ap())
    out = nc.dram_tensor("out_h", (TOK, P, D_MODEL), F32, kind="ExternalOutput").ap()
    build(nc, *args, out)
    result = run_bass_kernel_spmd(nc, [arrays], core_ids=[0])
    return result.results[0]["out_h"].reshape(1, SEQ, D_MODEL)
```
